# Optimizing a Trainium2 kernel written in Bass

```python
import jax, jax.numpy as jnp
from jax import lax
import numpy as np

D_MODEL = 2048
BATCH = 1
SEQ = 512
DEPTH = 1

GRID_W = 64
ROPE_THETA = 10000.0
RMS_EPS = 1e-6
Q_BLOCK = 128

N_HEADS_A = 8
N_KV_A = 2
HEAD_DIM_A = 128
GROUPS_A = N_HEADS_A // N_KV_A

N_HEADS_B = 8
Q_LORA = 512
KV_LORA = 512
NOPE_DIM_B = 128
ROPE_DIM_B = 64
V_DIM_B = 128
QK_DIM_B = NOPE_DIM_B + ROPE_DIM_B

D_FF = ((8 * D_MODEL // 3 + 255) // 256) * 256

PLE_DIM = 256

COL_SIZES = (
    N_HEADS_A * HEAD_DIM_A,
    N_KV_A * HEAD_DIM_A,
    N_KV_A * HEAD_DIM_A,
    Q_LORA,
    KV_LORA,
    ROPE_DIM_B,
    D_MODEL,
    D_MODEL,
)
IN_COLS = sum(COL_SIZES)
SPLITS = tuple(int(s) for s in np.cumsum(COL_SIZES)[:-1])

kernel_name = "hybrid_gqa_mla_gated_encoder_block"

def rmsnorm(x, g):
    x32 = x.astype(jnp.float32)
    y = x32 * lax.rsqrt(jnp.mean(x32 * x32, axis=-1, keepdims=True) + RMS_EPS)
    return (y * g.astype(jnp.float32)).astype(x.dtype)

def axial_angles(row, col, d):
    half = d // 2
    inv = 1.0 / (ROPE_THETA ** (jnp.arange(0, half, 2, dtype=jnp.float32) / half))
    return row[:, None] * inv[None, :], col[:, None] * inv[None, :]

def rotate(x, ang):
    n2 = x.shape[-1] // 2
    cos = jnp.cos(ang)[:, None, :].astype(x.dtype)
    sin = jnp.sin(ang)[:, None, :].astype(x.dtype)
    x1, x2 = x[..., :n2], x[..., n2:]
    return jnp.concatenate([x1 * cos - x2 * sin, x2 * cos + x1 * sin], axis=-1)

def axial_rope(x, ang_r, ang_c):
    half = x.shape[-1] // 2
    return jnp.concatenate([rotate(x[..., :half], ang_r), rotate(x[..., half:], ang_c)], axis=-1)

def block_attention(q, k, v, scale):
    b, s, hk, g, dk = q.shape
    nb = s // Q_BLOCK
    qb = q.reshape(b, nb, Q_BLOCK, hk, g, dk).transpose(1, 0, 2, 3, 4, 5)

    def one_block(qi):
        sc = jnp.einsum('bqhgd,bkhd->bhgqk', qi, k).astype(jnp.float32) * scale
        pr = jax.nn.softmax(sc, axis=-1).astype(v.dtype)
        return jnp.einsum('bhgqk,bkhd->bqhgd', pr, v)

    o = lax.map(one_block, qb)
    return o.transpose(1, 0, 2, 3, 4, 5).reshape(b, s, hk * g, v.shape[-1])

def setup_inputs(seed: int = 0) -> dict:
    key = jax.random.key(seed)
    ks = jax.random.split(key, 32)
    f32 = jnp.float32

    def w(k, shape, fan_in):
        return jax.random.normal(k, shape, f32) * (fan_in ** -0.5)

    def gain(k, n):
        return 1.0 + 0.02 * jax.random.normal(k, (DEPTH, n), f32)

    return {
        "x": jax.random.normal(ks[0], (BATCH, SEQ, D_MODEL), f32),
        "p": jax.random.normal(ks[1], (DEPTH, BATCH, SEQ, PLE_DIM), f32),
        "g_mix": gain(ks[2], D_MODEL),
        "w_in": w(ks[3], (DEPTH, D_MODEL, IN_COLS), D_MODEL),
        "q_norm_a": gain(ks[4], HEAD_DIM_A),
        "k_norm_a": gain(ks[5], HEAD_DIM_A),
        "q_a_norm": gain(ks[6], Q_LORA),
        "w_q_b": w(ks[7], (DEPTH, Q_LORA, N_HEADS_B * QK_DIM_B), Q_LORA),
        "kv_a_norm": gain(ks[8], KV_LORA),
        "w_kv_b": w(ks[9], (DEPTH, KV_LORA, N_HEADS_B * (NOPE_DIM_B + V_DIM_B)), KV_LORA),
        "w_a_out": w(ks[10], (DEPTH, N_HEADS_A * HEAD_DIM_A, D_MODEL), N_HEADS_A * HEAD_DIM_A),
        "w_b_out": w(ks[11], (DEPTH, N_HEADS_B * V_DIM_B, D_MODEL), N_HEADS_B * V_DIM_B),
        "w_o": w(ks[12], (DEPTH, D_MODEL, D_MODEL), D_MODEL),
        "g_ffn": gain(ks[13], D_MODEL),
        "w_gate_up": w(ks[14], (DEPTH, D_MODEL, 2 * D_FF), D_MODEL),
        "w_down": w(ks[15], (DEPTH, D_FF, D_MODEL), D_FF),
        "g_ple": gain(ks[16], D_MODEL),
        "w_ple_gate": w(ks[17], (DEPTH, D_MODEL, D_MODEL), D_MODEL),
        "w_ple_proj": w(ks[18], (DEPTH, PLE_DIM, D_MODEL), PLE_DIM),
        "g_ple_post": gain(ks[19], D_MODEL),
        "g_final": 1.0 + 0.02 * jax.random.normal(ks[20], (D_MODEL,), f32),
    }

def reference(x, p, g_mix, w_in, q_norm_a, k_norm_a, q_a_norm, w_q_b, kv_a_norm, w_kv_b,
              w_a_out, w_b_out, w_o, g_ffn, w_gate_up, w_down, g_ple, w_ple_gate,
              w_ple_proj, g_ple_post, g_final):
    b, s, _ = x.shape
    rows = s // GRID_W
    row = jnp.repeat(jnp.arange(rows, dtype=jnp.float32), GRID_W)
    col = jnp.tile(jnp.arange(GRID_W, dtype=jnp.float32), rows)
    ang_ra, ang_ca = axial_angles(row, col, HEAD_DIM_A)
    ang_rb, ang_cb = axial_angles(row, col, ROPE_DIM_B)

    h = x
    for i in range(DEPTH):
        u = rmsnorm(h, g_mix[i])
        z = u @ w_in[i]
        qa, ka, va, cq, ckv, kr, ga, gb = jnp.split(z, SPLITS, axis=-1)

        qa = rmsnorm(qa.reshape(b, s, N_HEADS_A, HEAD_DIM_A), q_norm_a[i])
        ka = rmsnorm(ka.reshape(b, s, N_KV_A, HEAD_DIM_A), k_norm_a[i])
        qa = axial_rope(qa, ang_ra, ang_ca)
        ka = axial_rope(ka, ang_ra, ang_ca)
        va = va.reshape(b, s, N_KV_A, HEAD_DIM_A)
        oa = block_attention(qa.reshape(b, s, N_KV_A, GROUPS_A, HEAD_DIM_A), ka, va,
                             HEAD_DIM_A ** -0.5)
        ya = oa.reshape(b, s, N_HEADS_A * HEAD_DIM_A) @ w_a_out[i]

        qb = (rmsnorm(cq, q_a_norm[i]) @ w_q_b[i]).reshape(b, s, N_HEADS_B, QK_DIM_B)
        q_nope, q_pe = qb[..., :NOPE_DIM_B], qb[..., NOPE_DIM_B:]
        q_pe = axial_rope(q_pe, ang_rb, ang_cb)
        kv = (rmsnorm(ckv, kv_a_norm[i]) @ w_kv_b[i]).reshape(b, s, N_HEADS_B, NOPE_DIM_B + V_DIM_B)
        k_nope, vb = kv[..., :NOPE_DIM_B], kv[..., NOPE_DIM_B:]
        k_pe = axial_rope(kr[:, :, None, :], ang_rb, ang_cb)
        k_pe = jnp.broadcast_to(k_pe, (b, s, N_HEADS_B, ROPE_DIM_B))
        q_full = jnp.concatenate([q_nope, q_pe], axis=-1)[:, :, :, None, :]
        k_full = jnp.concatenate([k_nope, k_pe], axis=-1)
        ob = block_attention(q_full, k_full, vb, QK_DIM_B ** -0.5)
        yb = ob.reshape(b, s, N_HEADS_B * V_DIM_B) @ w_b_out[i]

        merged = jax.nn.sigmoid(ga) * ya + jax.nn.sigmoid(gb) * yb
        h = h + merged @ w_o[i]

        gu = rmsnorm(h, g_ffn[i]) @ w_gate_up[i]
        g_, u_ = gu[..., :D_FF], gu[..., D_FF:]
        h = h + (jax.nn.silu(g_) * u_) @ w_down[i]

        e = rmsnorm(p[i] @ w_ple_proj[i], g_ple_post[i])
        gate = jax.nn.sigmoid(rmsnorm(h, g_ple[i]) @ w_ple_gate[i])
        h = h + gate * e

    return rmsnorm(h, g_final)


_drawn_inputs = setup_inputs


def setup_inputs(seed=0):
    import zlib

    import numpy as np

    out = dict(_drawn_inputs(seed))
    spreads = {}
    factors = {'g_mix': 8.0,
     'q_norm_a': 8.0,
     'k_norm_a': 8.0,
     'q_a_norm': 8.0,
     'kv_a_norm': 8.0,
     'g_ffn': 4.1,
     'g_ple': 64.0,
     'g_ple_post': 55.248,
     'g_final': 8.263}
    for name, (base, spread) in spreads.items():
        noise = np.random.default_rng([zlib.crc32(name.encode()), seed]).standard_normal(out[name].shape)
        drawn = base * np.exp(spread * noise) if base else spread * noise
        out[name] = __import__('jax').numpy.asarray(drawn.astype(out[name].dtype))
    for name, factor in factors.items():
        out[name] = (out[name] * factor).astype(out[name].dtype)
    return out
```

```python
from contextlib import ExitStack

import numpy as np

import concourse.bass as bass
from concourse import mybir

F32 = mybir.dt.float32
F32R = mybir.dt.float32r
ALU = mybir.AluOpType
ACT = mybir.ActivationFunctionType
AX_X = mybir.AxisListType.X

P = 128
SEQ = 512
D = 2048
KD = D // P
HEADS, KV_HEADS, HD = 8, 2, 128
GROUP = HEADS // KV_HEADS
LORA = 512
KL = LORA // P
ROPE_B = 64
QK_B = 128 + ROPE_B
D_FF = 5632
CHUNKS = D_FF // 512
PLE = 256
EPS = 1e-6
GRID_W = 64
THETA = 10000.0
COLS = 256
KP = 4
RAW = 4
HL = 2

C_Q, C_K, C_V = 0, 1024, 1280
C_CQ, C_CKV, C_KR = 1536, 2048, 2560
C_GA, C_GB = 2624, 4672

N_QKV, N_GATE = 0, 28
N_LAT = N_GATE + 8 * 8
N_B = N_LAT + 16
N_MERGE = N_B + 16
N_WO = N_MERGE + 32
N_FF = N_WO + 32
N_FF_LOOP = N_FF + 4
N_FF_LAST = N_FF_LOOP + 24 * (CHUNKS - 1)
N_E = N_FF_LAST + 12
N_D = N_E + 8
N_PLE = N_D + 8
N_END = N_PLE + 32
G_GATE = 7
G_LAT = G_GATE + 16
G_B = G_LAT + 4
G_MERGE = G_B + 16
G_WO = G_MERGE + 16
G_FF = G_WO + 8
G_FF_LOOP = G_FF + 1
G_FF_LAST = G_FF_LOOP + 12 * (CHUNKS - 1)
G_E = G_FF_LAST + 3
G_D = G_E + 8
G_PLE = G_D + 8
G_END = G_PLE + 8

G_MIX, G_FFN, G_PLEN, G_POST, G_FIN, G_QA, G_KVA, G_QN, G_KN = 0, 16, 32, 48, 64, 80, 84, 88, 89
GAINS = 90

OP_K, OP_Q0, OP_V, OP_KR, OP_B = 0, 2, 3, 12, 13


def build(nc, xT, pT, gains, tables, mats, w_in, w_qb, w_kvb, w_a, w_b, w_o, w_gu, w_dn, w_pg, w_pp, outT):
    with ExitStack() as ctx:
        def sb(name, shape, dt=F32):
            return ctx.enter_context(nc.sbuf_tensor(name, shape, dt))

        def sem(name):
            return ctx.enter_context(nc.semaphore(name))

        raw = sb("raw", [P, RAW, KP, COLS])
        w_hi = sb("w_hi", [P, HL, KP, COLS], F32R)
        w_lo = sb("w_lo", [P, HL, KP, COLS], F32R)
        res = sb("res", [P, KD, SEQ])
        tmp = sb("tmp", [P, 4, SEQ])
        tab = sb("tab", [P, 4, SEQ])
        acc = sb("acc", [P, SEQ])
        rstd = sb("rstd", [P, 3, SEQ])
        cm = sb("cm", [P, 4, P])
        gn = sb("gn", [P, GAINS])
        eps = sb("eps", [P, 1])
        negmax = sb("negmax", [P, 4])
        psumrow = sb("psumrow", [P, 4])
        rrow = sb("rrow", [P, 4])
        r0 = sb("r0", [P, 8, 2, SEQ], F32R)
        r1 = sb("r1", [P, 8, 2, SEQ], F32R)
        r3 = sb("r3", [P, 8, 2, SEQ], F32R)
        with nc.sbuf_tensor("r2", [P, 8, 2, SEQ], F32R) as r2:
            pass
        emb = sb("emb", [P, KD, SEQ])
        ident, ones, swap_a, swap_b = (cm[:, i, :] for i in range(4))
        ps = ctx.enter_context(nc.psum_tensor("ps", [P, 8, SEQ], F32))
        gates = nc.dram_tensor("gates", [2, KD, P, SEQ], F32, kind="Internal").ap()

        raw_in = [sem(f"raw_in{i}") for i in range(RAW)]
        w_hi_done, w_lo_done, piece_used = sem("w_hi_done"), sem("w_lo_done"), sem("piece_used")
        emptied = sem("emptied")
        x_in = [sem(f"x_in{i}") for i in range(4)]
        x_again = [sem(f"x_again{i}") for i in range(2)]
        const_in, p_in = sem("const_in"), sem("p_in")
        gate_in = [sem(f"gate_in{i}") for i in range(2)]
        gate_out = [sem(f"gate_out{i}") for i in range(2)]
        u_hi, u_lo = sem("u_hi"), sem("u_lo")
        sq_done, acc_done, tot_done = sem("sq_done"), sem("acc_done"), sem("tot_done")
        root_done, rstd_done = sem("root_done"), sem("rstd_done")
        hsq, htot, hroot, hrecip, hnorm = sem("hsq"), sem("htot"), sem("hroot"), sem("hrecip"), sem("hnorm")
        swapped, by_cos, by_sin, roped = sem("swapped"), sem("by_cos"), sem("by_sin"), sem("roped")
        v_turned, op_hi, op_lo = sem("v_turned"), sem("op_hi"), sem("op_lo")
        scores, max_done, exp_done, rsum_done, p_done = (sem("scores"), sem("max_done"), sem("exp_done"),
                                                         sem("rsum_done"), sem("p_done"))
        p_turned, pt_hi, pt_lo, pv_done = sem("p_turned"), sem("pt_hi"), sem("pt_lo"), sem("pv_done")
        o_hi, o_lo = sem("o_hi"), sem("o_lo")
        gate_pre, gate_sig = sem("gate_pre"), sem("gate_sig")
        lat_pre = sem("lat_pre")
        mrg_a, mrg_sum, mrg_hi, mrg_lo = sem("mrg_a"), sem("mrg_sum"), sem("mrg_hi"), sem("mrg_lo")
        res_done = sem("res_done")
        ff_pre, ff_act, ff_mul, ff_hi, ff_lo = sem("ff_pre"), sem("ff_act"), sem("ff_mul"), sem("ff_hi"), sem("ff_lo")
        emb_done, emb_normed = sem("emb_done"), sem("emb_normed")
        pg_pre, pg_sig, pg_mul, pg_res = sem("pg_pre"), sem("pg_sig"), sem("pg_mul"), sem("pg_res")
        fin_scaled, fin_done, out_done = sem("fin_scaled"), sem("fin_done"), sem("out_done")
        set_done = sem("set_done")

        def u_tile(k):
            return (r0 if k < 8 else r1)[:, k % 8]

        def m_tile(k):
            return (r1 if k < 8 else r2)[:, k % 8]

        def sums(norm):
            return tab[:, 3, :] if norm == 4 else acc[:]

        def n_tile(k):
            return (r3 if k < 8 else r0)[:, k % 8]

        K_A, V_A, Q_A = [r2[:, 0], r2[:, 1]], [r2[:, 2], r2[:, 3]], r2[:, 4]
        PT_A = [r2[:, 5], r2[:, 6]]
        Q_B, PE_B, K_B, V_B, KR_B = (r1[:, i] for i in range(5))
        PT_B = [r1[:, 5], r1[:, 6]]
        P_T = [r1[:, 4], r1[:, 5]]
        PROB = 8

        block = ctx.enter_context(nc.Block())

        @block.sync
        def _(sp):
            def load(n, j, w, k0, col, kt=KP, cols=COLS):
                src = w[k0 * P:(k0 + kt) * P, :].rearrange("(k p) c -> p k c", p=P)[:, :, bass.ds(col, cols)]
                if kt == KP:
                    dst = raw[:, j, :, 0:cols]
                else:
                    dst = raw[:, j, 0:kt, 0:cols]
                if not isinstance(n, int) or n >= RAW:
                    sp.wait_ge(w_lo_done, n - RAW + 1)
                sp.dma_start(dst, src).then_inc(raw_in[j], 16)

            x_v = xT.rearrange("(k p) s -> p k s", p=P)
            load(0, 0, w_in, 0, C_K)
            sp.dma_start(res[:, 0:4, :], x_v[:, 0:4, :]).then_inc(x_in[0], 16)
            sp.dma_start(gn[:], gains).then_inc(const_in, 16)
            load(1, 1, w_in, 4, C_K)
            sp.dma_start(res[:, 4:8, :], x_v[:, 4:8, :]).then_inc(x_in[1], 16)
            load(2, 2, w_in, 8, C_K)
            sp.dma_start(res[:, 8:12, :], x_v[:, 8:12, :]).then_inc(x_in[2], 16)
            load(3, 3, w_in, 12, C_K)
            sp.dma_start(res[:, 12:16, :], x_v[:, 12:16, :]).then_inc(x_in[3], 16)
            sp.dma_start(cm[:], mats).then_inc(const_in, 16)
            sp.dma_start(tab[:], tables).then_inc(const_in, 16)
            n = 4
            for col in [C_V, C_Q, C_Q + 256, C_Q + 512, C_Q + 768, C_KR]:
                for j in range(4):
                    load(n + j, j, w_in, 4 * j, col)
                n += 4
            with sp.Fori(0, HEADS) as h:
                ca, cb = sp.snap(h * COLS + C_GA), sp.snap(h * COLS + C_GB)
                for j in range(8):
                    load(h * 8 + N_GATE + j, j % 4, w_in, 4 * (j % 4), ca if j < 4 else cb)
            for g in range(4):
                for j in range(4):
                    load(N_LAT + 4 * g + j, j, w_in, 4 * j, C_CQ + COLS * g)
            with sp.Fori(0, HEADS // 2) as i:
                for s in range(2):
                    cq, ckv = sp.snap(i * (2 * QK_B) + s * QK_B), sp.snap(i * (2 * COLS) + s * COLS)
                    load(i * 4 + N_B + 2 * s, 2 * s, w_qb, 0, cq, cols=QK_B)
                    load(i * 4 + N_B + 2 * s + 1, 2 * s + 1, w_kvb, 0, ckv)
            x_tiles = xT.rearrange("(k p) s -> p k s", p=P)
            with sp.Fori(0, 4) as i:
                for s in range(2):
                    col = sp.snap(i * (2 * COLS) + s * COLS)
                    t = sp.snap(i * 4 + 2 * s)
                    for b, w in enumerate((w_a, w_b)):
                        for j in range(2):
                            load(i * 8 + N_MERGE + 4 * s + 2 * b + j, 2 * b + j, w, 4 * j, col)
                    sp.wait_ge(gate_out[0], 16 * HEADS)
                    sp.wait_ge(gate_out[1], 16 * HEADS)
                    sp.wait_ge(p_turned, 8 * HEADS)
                    sp.wait_ge(emptied, i * 4 + 2 * s + G_MERGE - 2)
                    for b in range(2):
                        sp.dma_start(res[:, 8 + 4 * s + 2 * b:10 + 4 * s + 2 * b, :],
                                     gates[b].rearrange("k p s -> p k s")[:, bass.ds(t, 2), :]
                                     ).then_inc(gate_in[s], 16)
            sp.wait_ge(op_lo, OP_B + 4 * HEADS)
            sp.dma_start(res[:, 0:8, :], x_tiles[:, 0:8, :]).then_inc(x_again[0], 16)
            for j in range(4):
                load(N_WO + j, j, w_o, 4 * j, 0)
            sp.wait_ge(emptied, G_WO)
            sp.dma_start(res[:, 8:16, :], x_tiles[:, 8:16, :]).then_inc(x_again[1], 16)
            with sp.Fori(1, 8) as g:
                col = sp.snap(g * COLS)
                for j in range(4):
                    load(g * 4 + N_WO + j, j, w_o, 4 * j, col)

            def group4(n, w, col):
                for j in range(4):
                    load(n + j, j, w, 4 * j, col)

            def down_rows(n, row):
                for d in range(8):
                    src = w_dn[bass.ds(row, 512), d * COLS:(d + 1) * COLS].rearrange("(k p) c -> p k c", p=P)
                    sp.wait_ge(w_lo_done, n + d - RAW + 1)
                    sp.dma_start(raw[:, d % 4], src).then_inc(raw_in[d % 4], 16)

            sp.dma_start(tab[:, 2:4, :], pT.rearrange("(k p) s -> p k s", p=P)).then_inc(p_in, 16)
            group4(N_FF, w_gu, 0)
            with sp.Fori(0, CHUNKS - 1) as c:
                cols = [sp.snap(c * 512 + off) for off in (D_FF, 256, D_FF + 256, 512)]
                row = sp.snap(c * 512)
                for g in range(4):
                    group4(c * 24 + N_FF_LOOP + 4 * g, w_gu, cols[g])
                down_rows(c * 24 + N_FF_LOOP + 16, row)
            last = 512 * (CHUNKS - 1)
            for g, off in enumerate((D_FF, 256, D_FF + 256)):
                group4(N_FF_LAST + 4 * g, w_gu, last + off)
            for g in range(8):
                load(N_E + g, g % 4, w_pp, 0, COLS * g, kt=2)
            down_rows(N_D, last)
            with sp.Fori(0, 8) as g:
                col = sp.snap(g * COLS)
                for j in range(4):
                    load(g * 4 + N_PLE + j, j, w_pg, 4 * j, col)
            o_v = outT.rearrange("(k p) s -> p k s", p=P)
            for t in range(0, KD, 2):
                sp.wait_ge(fin_done, t + 2)
                sp.dma_start(o_v[:, t:t + 2, :], res[:, t:t + 2, :]).then_inc(out_done, 16)
            sp.wait_ge(out_done, 16 * KD // 2)

        @block.tensor
        def _(pe):
            mm = nc.tensor.matmul

            def product(out, hi, lo, x, start, stop):
                mm(out, hi, x[:, 0, :], start=start, stop=False)
                mm(out, hi, x[:, 1, :], start=False, stop=False)
                return mm(out, lo, x[:, 0, :], start=False, stop=stop)

            def piece(n, j, bank, xs, first, last, tiles=2):
                pe.wait_ge(w_lo_done, n + 1)
                s = j % HL
                for k, x in enumerate(xs):
                    for t in range(tiles):
                        i = product(ps[:, bank + t, :], w_hi[:, s, k, P * t:P * t + P], w_lo[:, s, k, P * t:P * t + P],
                                    x, first and k == 0, last and k == len(xs) - 1)
                i.then_inc(piece_used, 1)

            def free(g, lag=2):
                if not isinstance(g, int) or g >= lag:
                    pe.wait_ge(emptied, g - lag + 1)

            def total(norm, bank):
                pe.wait_ge(acc_done, [16, 20, 24, 40, 56, 72, 88][norm])
                mm(ps[:, bank, :], ones, sums(norm), start=True, stop=True).then_inc(tot_done, 1)

            def head_total(m):
                pe.wait_ge(hsq, m + 1)
                if not isinstance(m, int) or m > 0:
                    pe.wait_ge(by_sin, m)
                mm(ps[:, 7:8, :], ones, res[:, 13:14, :], start=True, stop=True).then_inc(htot, 1)

            def head_swap(m, tile):
                pe.wait_ge(hnorm, m + 1)
                mm(ps[:, 7:8, :], swap_a, tile, start=True, stop=True).then_inc(swapped, 1)

            def turn_v(tile, bank):
                for kt in range(4):
                    i = nc.tensor.transpose(ps[:, bank, kt * P:(kt + 1) * P], tile[:, kt * P:(kt + 1) * P], ident)
                i.then_inc(v_turned, 1)

            def score(n, q_ops, k_ops, need, need_last):
                pe.wait_ge(op_lo, need)
                for q in range(4):
                    if q == 2 and not (isinstance(n, int) and n == 0):
                        pe.wait_ge(o_lo, n)
                    if q == 3:
                        pe.wait_ge(op_lo, need_last)
                    for i, (qo, ko) in enumerate(zip(q_ops, k_ops)):
                        last = product(ps[:, 4 + q, :], qo[:, 0, q * P:(q + 1) * P], qo[:, 1, q * P:(q + 1) * P],
                                       ko, i == 0, i == len(q_ops) - 1)
                    last.then_inc(scores, 1)

            def turn_p(n, kt):
                if kt == 0:
                    pe.wait_ge(p_done, n * 4 + 4)
                if kt >= 2:
                    pe.wait_ge(pt_lo, n * 4 + kt - 1)
                for q in range(4):
                    i = nc.tensor.transpose(ps[:, 4 + kt % 2, q * P:(q + 1) * P],
                                            res[:, PROB + q, kt * P:(kt + 1) * P], ident)
                i.then_inc(p_turned, 1)

            def weigh(n, kt, v, pt):
                pe.wait_ge(pt_lo, n * 4 + kt + 1)
                if kt == 0 and not (isinstance(n, int) and n == 0):
                    pe.wait_ge(o_lo, n)
                product(ps[:, 6, :], v[:, 0, kt * P:(kt + 1) * P], v[:, 1, kt * P:(kt + 1) * P], pt[kt % 2],
                        kt == 0, kt == 3).then_inc(pv_done, 1)

            pe.wait_ge(const_in, 48)
            def in_group(g, b, pair):
                free(g)
                for j in range(4):
                    piece(b + j, j, 2 * pair, [u_tile(4 * j + k) for k in range(4)], j == 0, j == 3)

            for j in range(4):
                pe.wait_ge(u_lo, 4 * j + 4)
                piece(j, j, 0, [u_tile(4 * j + k) for k in range(4)], j == 0, j == 3)
            total(0, 7)
            in_group(1, 4, 1)
            with pe.Fori(0, 2) as i:
                in_group(i * 2 + 2, i * 8 + 8, 0)
                in_group(i * 2 + 3, i * 8 + 12, 1)
            free(6)
            pe.wait_ge(root_done, 1)
            for j in range(4):
                if j < 3:
                    head_total(j)
                piece(24 + j, j, 0, [u_tile(4 * j + k) for k in range(4)], j == 0, j == 3, tiles=1)
                if j < 3:
                    head_swap(j, res[:, [8, 9, 0][j]:[9, 10, 1][j], :])
                if j == 2:
                    turn_v(res[:, 10, :], 4)
                    turn_v(res[:, 11, :], 5)

            def gqa_head(h, kv, more):
                b = h * 8 + N_GATE
                score(h, [Q_A], [K_A[kv]], h + 5, h + 5)
                xs = [[u_tile(4 * j + k) for k in range(4)] for j in range(4)]
                free(h * 2 + G_GATE)
                for j in range(4):
                    piece(b + j, j, 2, xs[j], j == 0, j == 3)
                turn_p(h, 0)
                turn_p(h, 1)
                free(h * 2 + G_GATE + 1)
                piece(b + 4, 4, 0, xs[0], True, False)
                weigh(h, 0, V_A[kv], PT_A)
                weigh(h, 1, V_A[kv], PT_A)
                turn_p(h, 2)
                turn_p(h, 3)
                piece(b + 5, 5, 0, xs[1], False, False)
                weigh(h, 2, V_A[kv], PT_A)
                weigh(h, 3, V_A[kv], PT_A)
                if more:
                    head_total(h + 3)
                piece(b + 6, 6, 0, xs[2], False, False)
                if more:
                    head_swap(h + 3, res[:, bass.ds(h + 1, 1), :])
                piece(b + 7, 7, 0, xs[3], False, True)

            gqa_head(0, 0, True)
            with pe.Fori(1, GROUP) as h:
                gqa_head(h, 0, True)
            with pe.Fori(GROUP, HEADS - 1) as h:
                gqa_head(h, 1, True)
            gqa_head(HEADS - 1, 1, False)

            for g in range(4):
                free(G_LAT + g)
                for j in range(4):
                    piece(N_LAT + 4 * g + j, j, 2 * ((G_LAT + g) % 2), [u_tile(4 * j + k) for k in range(4)],
                          j == 0, j == 3)
                if g == 2:
                    total(1, 6)

            def mla_up(h):
                b = h * 2 + N_B
                free(h * 2 + G_B)
                piece(b, 0, 2, [r2[:, k] for k in range(4)], True, True)
                free(h * 2 + G_B + 1)
                piece(b + 1, 1, 0, [r2[:, 4 + k] for k in range(4)], True, True)

            def pe_swap(m, src, need):
                pe.wait_ge(emptied, need)
                mm(ps[:, 7, :], swap_b[0:ROPE_B, :], src, start=True, stop=True).then_inc(swapped, 1)

            pe.wait_ge(u_lo, 24)
            pe_swap(10, res[0:ROPE_B, 12, :], 7)
            free(G_B)
            piece(N_B, 0, 2, [r2[:, k] for k in range(4)], True, True)
            pe.wait_ge(by_sin, 11)
            total(2, 7)
            free(G_B + 1)
            piece(N_B + 1, 1, 0, [r2[:, 4 + k] for k in range(4)], True, True)
            pe.wait_ge(root_done, 3)
            pe_swap(11, res[0:ROPE_B, 1, :], G_B + 1)
            pe.wait_ge(by_sin, 12)
            pe.wait_ge(emptied, G_B + 2)
            turn_v(res[:, 3, :], 7)

            def mla_head(h, more):
                n = h + HEADS
                score(n, [Q_B, PE_B_64], [K_B, KR_B_64], h * 4 + OP_B + 3, h * 4 + OP_B + 4)
                if more:
                    mla_up(h + 1)
                turn_p(n, 0)
                turn_p(n, 1)
                if more:
                    pe_swap(h + 12, res[0:ROPE_B, 1, :], h * 2 + G_B + 3)
                weigh(n, 0, V_B, PT_B)
                weigh(n, 1, V_B, PT_B)
                turn_p(n, 2)
                turn_p(n, 3)
                if more:
                    pe.wait_ge(by_sin, h + 13)
                    pe.wait_ge(emptied, h * 2 + G_B + 4)
                    turn_v(res[:, 3, :], 7)
                weigh(n, 2, V_B, PT_B)
                weigh(n, 3, V_B, PT_B)

            PE_B_64, KR_B_64 = PE_B[0:ROPE_B], KR_B[0:ROPE_B]
            with pe.Fori(0, HEADS - 1) as h:
                mla_head(h, True)
            mla_head(HEADS - 1, False)

            with pe.Fori(0, 4) as i:
                for s in range(2):
                    for b, r in enumerate((r3, r0)):
                        free(i * 4 + G_MERGE + 2 * s + b)
                        pe.wait_ge(o_lo, 16)
                        for j in range(2):
                            piece(i * 8 + N_MERGE + 4 * s + 2 * b + j, j, 2 * (1 - b),
                                  [r[:, 4 * j + k] for k in range(4)], j == 0, j == 1)

            with pe.Fori(0, 4) as i:
                for s in range(2):
                    free(i * 2 + G_WO + s)
                    for j in range(4):
                        pe.wait_ge(mrg_lo, 2 * j + 2)
                        piece(i * 8 + N_WO + 4 * s + j, j, 2 * (1 - s), [m_tile(4 * j + k) for k in range(4)],
                              j == 0, j == 3)

            def n_group(g, n, pair, lag=4):
                free(g, lag)
                for j in range(4):
                    piece(n + j, j, 2 * pair, [n_tile(4 * j + k) for k in range(4)], j == 0, j == 3)

            def down(g, n, pair0, need):
                pe.wait_ge(ff_lo, need)
                for d in range(8):
                    free(g + d, 4)
                    piece(n + d, d, 2 * ((pair0 + d) % 4), [r1[:, k] for k in range(4)], True, True)

            pe.wait_ge(emptied, G_FF)
            for j in range(4):
                pe.wait_ge(u_lo, 24 + 4 * j + 4)
                piece(N_FF + j, j, 0, [n_tile(4 * j + k) for k in range(4)], j == 0, j == 3)
            total(3, 7)
            n_group(G_FF + 1, N_FF_LOOP, 1)
            n_group(G_FF + 2, N_FF_LOOP + 4, 2)
            pe.wait_ge(root_done, 4)
            n_group(G_FF + 3, N_FF_LOOP + 8, 3)
            with pe.Fori(0, CHUNKS - 2) as c:
                n_group(c * 12 + G_FF + 4, c * 24 + N_FF_LOOP + 12, 0)
                down(c * 12 + G_FF + 5, c * 24 + N_FF_LOOP + 16, 1, c * 2 + 2)
                for g in range(3):
                    n_group(c * 12 + G_FF + 13 + g, c * 24 + N_FF_LOOP + 24 + 4 * g, 1 + g)
            c = CHUNKS - 2
            n_group(c * 12 + G_FF + 4, c * 24 + N_FF_LOOP + 12, 0)
            down(c * 12 + G_FF + 5, c * 24 + N_FF_LOOP + 16, 1, c * 2 + 2)
            for g in range(3):
                n_group(G_FF_LAST + g, N_FF_LAST + 4 * g, 1 + g)
            pe.wait_ge(u_lo, 42)
            with pe.Fori(0, 2) as i:
                for s in range(4):
                    free(i * 4 + G_E + s, 4)
                    piece(i * 4 + N_E + s, s, 2 * s, P_T, True, True)
            down(G_D, N_D, 0, 2 * CHUNKS)
            free(G_PLE, 4)
            for j in range(4):
                pe.wait_ge(u_lo, 42 + 4 * j + 4)
                piece(N_PLE + j, j, 0, [n_tile(4 * j + k) for k in range(4)], j == 0, j == 3)
            free(G_PLE + 3, 4)
            total(4, 6)
            total(5, 7)
            n_group(G_PLE + 1, N_PLE + 4, 1)
            n_group(G_PLE + 2, N_PLE + 8, 2)
            pe.wait_ge(root_done, 6)
            n_group(G_PLE + 3, N_PLE + 12, 3)
            for g in range(4, 8):
                n_group(G_PLE + g, N_PLE + 4 * g, g % 4)
            pe.wait_ge(emptied, G_END)
            total(6, 7)

        @block.scalar
        def _(act):
            def copy(out, in_, scale=1.0):
                return nc.scalar.activation(out, in_, ACT.Copy, scale=scale)

            def whi(n, j):
                count = (n - j) * 4 + 16
                act.wait_ge(raw_in[j], count)
                if not isinstance(n, int) or n >= HL:
                    act.wait_ge(piece_used, n - HL + 1)
                copy(w_hi[:, j % HL], raw[:, j]).then_inc(w_hi_done, 1)

            def square(s, tile, sq, need, count):
                act.wait_ge(need, count)
                if s >= 2:
                    act.wait_ge(acc_done, s - 1)
                nc.scalar.activation(sq[:, s % 2, :], tile, ACT.Square).then_inc(sq_done, 1)

            def root(norm, bank, dst, width):
                act.wait_ge(tot_done, norm + 1)
                nc.scalar.activation(rstd[:, dst, :], ps[:, bank, :], ACT.Sqrt, scale=1.0 / width,
                                     bias=eps[:]).then_inc(root_done, 1)

            sq_a = tmp[:, 2:4, :]
            sq_b = tab[:, 0:2, :]

            def head_square(m, tile, need, count):
                act.wait_ge(need, count)
                nc.scalar.activation(res[:, 13:14, :], tile, ACT.Square).then_inc(hsq, 1)

            def head_root(m):
                act.wait_ge(htot, m + 1)
                if not isinstance(m, int) or m > 0:
                    act.wait_ge(roped, m)
                nc.scalar.activation(res[:, 14, :], ps[:, 7, :], ACT.Sqrt, scale=1.0 / HD,
                                     bias=eps[:]).then_inc(hroot, 1)

            def op_split(out, in_, scale=1.0):
                copy(out[:, 0, :], in_, scale).then_inc(op_hi, 1)

            SA, SB = float(HD) ** -0.5, float(QK_B) ** -0.5

            def exps(n):
                for q in range(4):
                    act.wait_ge(max_done, n * 4 + q + 1)
                    if q == 0 and not (isinstance(n, int) and n == 0):
                        act.wait_ge(p_turned, n * 4)
                    nc.scalar.activation(res[:, PROB + q, :], ps[:, 4 + q, :], ACT.Exp, bias=negmax[:, q:q + 1],
                                         accum_out=psumrow[:, q:q + 1]).then_inc(exp_done, 1)

            def pt_split(n, kt, pt):
                act.wait_ge(p_turned, n * 4 + kt + 1)
                if kt >= 2 or not (isinstance(n, int) and n == 0):
                    act.wait_ge(pv_done, n * 4 + kt - 1)
                copy(pt[kt % 2][:, 0, :], ps[:, 4 + kt % 2, :]).then_inc(pt_hi, 1)

            def o_split(n, out):
                act.wait_ge(pv_done, n * 4 + 4)
                copy(out, ps[:, 6:7, :]).then_inc(o_hi, 1)

            nc.scalar.preload_act_table(ACT.Sigmoid)
            act.wait_ge(set_done, 1)
            act.wait_ge(const_in, 48)
            for k in range(KD):
                if k % 4 == 0:
                    if k < 8:
                        whi(k // 4, k // 4)
                    act.wait_ge(x_in[k // 4], 16)
                if k == 8:
                    whi(2, 2)
                if k == 12:
                    whi(3, 3)
                copy(u_tile(k)[:, 0, :], res[:, k, :], gn[:, G_MIX + k:G_MIX + k + 1]).then_inc(u_hi, 1)
                square(k, res[:, k, :], sq_a, u_hi, k + 1)
            whi(4, 0)
            whi(5, 1)
            root(0, 7, 0, D)
            for g in range(1, 6):
                for j in range(4):
                    whi(4 * g + 2 + j, (2 + j) % 4)
            head_square(0, res[:, 8:9, :], emptied, 3)
            for m in range(3):
                head_root(m)
                if m < 2:
                    head_square(m + 1, res[:, [9, 0][m]:[10, 1][m], :], htot, m + 1)
                act.wait_ge(roped, m + 1)
                op_split([K_A[0], K_A[1], Q_A][m], res[:, 15, :], SA if m == 2 else 1.0)
                whi(26 + m, (2 + m) % 4)
            for v in range(2):
                act.wait_ge(v_turned, v + 1)
                op_split(V_A[v], ps[:, 4 + v, :])
            whi(29, 1)

            def gate_sigmoid(h, branch):
                t = tmp[:, 2 * branch:2 * branch + 2, :]
                act.wait_ge(emptied, h * 2 + G_GATE + branch + 1)
                nc.scalar.activation(t, t, ACT.Sigmoid).then_inc(gate_sig, 1)
                act.wait_ge(gate_sig, h * 2 + branch + 1)
                act.dma_start(gates[branch].rearrange("k p s -> p k s")[:, bass.ds(h * 2, 2), :],
                              t).then_inc(gate_out[branch], 16)

            def gqa_head(h, kv, more):
                b = h * 8 + N_GATE
                exps(h)
                if more:
                    head_square(h + 3, res[:, bass.ds(h + 1, 1), :], htot, h + 3)
                for j in range(4):
                    whi(b + 2 + j, (2 + j) % 4)
                gate_sigmoid(h, 0)
                pt_split(h, 0, PT_A)
                pt_split(h, 1, PT_A)
                whi(b + 6, 2)
                pt_split(h, 2, PT_A)
                pt_split(h, 3, PT_A)
                whi(b + 7, 3)
                o_split(h, r3[:, bass.ds(h, 1), 0, :])
                if more:
                    head_root(h + 3)
                whi(b + 8, 0)
                if more:
                    act.wait_ge(roped, h + 4)
                    op_split(Q_A, res[:, 15, :], SA)
                whi(b + 9, 1)
                gate_sigmoid(h, 1)

            gqa_head(0, 0, True)
            with act.Fori(1, GROUP) as h:
                gqa_head(h, 0, True)
            with act.Fori(GROUP, HEADS - 1) as h:
                gqa_head(h, 1, True)
            gqa_head(HEADS - 1, 1, False)

            act.wait_ge(gate_out[1], 16 * HEADS)
            for g in range(4):
                for j in range(4):
                    whi(N_LAT + 4 * g + 2 + j, (2 + j) % 4)
                for t in range(2):
                    k = 2 * g + t
                    act.wait_ge(emptied, G_LAT + g + 1)
                    copy(r2[:, k, 0, :], tmp[:, t, :], gn[:, G_QA + k:G_QA + k + 1]).then_inc(u_hi, 1)
                    square(16 + k, tmp[:, t, :], sq_a, emptied, G_LAT + g + 1)
                if g == 2:
                    root(1, 6, 1, LORA)
            act.wait_ge(roped, 11)
            copy(KR_B[0:ROPE_B, 0, :], res[0:ROPE_B, 6, :]).then_inc(op_hi, 1)
            root(2, 7, 2, LORA)

            def mla_prep(h, bn, bk):
                act.wait_ge(emptied, h * 2 + G_B + 1)
                act.wait_ge(scores, h * 4 + 32)
                op_split(Q_B, res[:, 0, :], SB)
                bn()
                act.wait_ge(emptied, h * 2 + G_B + 2)
                op_split(K_B, res[:, 2, :])
                bk()
                act.wait_ge(roped, h + 12)
                copy(PE_B[0:ROPE_B, 0, :], res[0:ROPE_B, 6, :], SB).then_inc(op_hi, 1)

            def mla_v(h):
                act.wait_ge(v_turned, h + 3)
                op_split(V_B, ps[:, 7, :])

            whi(N_B + 2, 2)
            mla_prep(0, lambda: whi(N_B + 3, 3), lambda: None)
            mla_v(0)

            def mla_head(h, j0, more):
                n = h + HEADS
                b = h * 2 + N_B + 4
                exps(n)
                if more:
                    whi(b, j0)
                    mla_prep(h + 1, lambda: whi(b + 1, j0 + 1), lambda: (pt_split(n, 0, PT_B), pt_split(n, 1, PT_B)))
                else:
                    pt_split(n, 0, PT_B)
                    pt_split(n, 1, PT_B)
                pt_split(n, 2, PT_B)
                pt_split(n, 3, PT_B)
                if more:
                    act.wait_ge(pv_done, n * 4 + 4)
                    mla_v(h + 1)
                o_split(n, r0[:, bass.ds(h, 1), 0, :])

            with act.Fori(0, HEADS // 2 - 1) as i:
                mla_head(i * 2, 0, True)
                mla_head(i * 2 + 1, 2, True)
            mla_head(HEADS - 2, 0, True)
            mla_head(HEADS - 1, 2, False)

            def merge(half, i, s):
                pair = i * 2 + half * 4 + s
                for j in range(2):
                    whi(pair * 4 + N_MERGE + 2 + j, 2 + j)
                for j in range(2):
                    whi(pair * 4 + N_MERGE + 4 + j, j)
                r = r1 if half == 0 else r2
                act.wait_ge(mrg_sum, pair + 1)
                copy(r[:, bass.ds(i * 4 + 2 * s, 2), 0, :], tmp[:, 0:2, :]).then_inc(mrg_hi, 1)

            for half in range(2):
                with act.Fori(0, 2) as i:
                    merge(half, i, 0)
                    merge(half, i, 1)

            for g in range(8):
                for j in range(4):
                    whi(N_WO + 4 * g + 2 + j, (2 + j) % 4)
                for t in range(2):
                    k = 2 * g + t
                    act.wait_ge(emptied, G_WO + g + 1)
                    copy(n_tile(k)[:, 0, :], res[:, k, :], gn[:, G_FFN + k:G_FFN + k + 1]).then_inc(u_hi, 1)
                    square(24 + k, res[:, k, :], sq_b, emptied, G_WO + g + 1)

            def ff_gate(g):
                act.wait_ge(emptied, g + 1)
                nc.scalar.activation(tmp[:, 0:2, :], tmp[:, 0:2, :], ACT.Silu).then_inc(ff_act, 1)

            def ff_hidden(e, half, down_before):
                act.wait_ge(ff_mul, e + 1)
                act.wait_ge(piece_used, down_before)
                copy(r1[:, 2 * half:2 * half + 2, 0, :], tmp[:, 2:4, :]).then_inc(ff_hi, 1)

            def four(n):
                for j in range(4):
                    whi(n + 2 + j, (2 + j) % 4)

            four(N_FF)
            root(3, 7, 0, D)
            nc.scalar.preload_act_table(ACT.Silu)
            ff_gate(G_FF)
            act.wait_ge(p_in, 16)
            for k in range(2):
                copy(P_T[k][:, 0, :], tab[:, 2 + k, :]).then_inc(u_hi, 1)

            def chunk(c, last):
                b, g = c * 24 + N_FF_LOOP, c * 12 + G_FF
                four(b)
                whi(b + 6, 2)
                ff_hidden(c * 2, 0, b)
                for j in range(3):
                    whi(b + 7 + j, (3 + j) % 4)
                ff_gate(g + 2)
                four(b + 8)
                if not last:
                    whi(b + 14, 2)
                    ff_hidden(c * 2 + 1, 1, b)
                    for j in range(3):
                        whi(b + 15 + j, (3 + j) % 4)
                    ff_gate(g + 4)
                    for d in range(8):
                        whi(b + 18 + d, (2 + d) % 4)
                else:
                    for i in range(8):
                        whi(b + 14 + i, (2 + i) % 4)
                        if i == 1:
                            ff_hidden(c * 2 + 1, 1, b)
                        for t in range(2):
                            k = 2 * i + t
                            square(40 + k, emb[:, k, :], sq_b, emptied, G_E + i + 1)

            with act.Fori(0, CHUNKS - 1) as c:
                chunk(c, False)
            chunk(CHUNKS - 1, True)
            for d in range(8):
                whi(N_D + d + 2, (2 + d) % 4)
                for t in range(2):
                    k = 2 * d + t
                    act.wait_ge(emptied, G_D + d + 1)
                    copy(n_tile(k)[:, 0, :], res[:, k, :], gn[:, G_PLEN + k:G_PLEN + k + 1]).then_inc(u_hi, 1)
                    square(56 + k, res[:, k, :], sq_b, emptied, G_D + d + 1)
            for g in range(8):
                for j in range(4 if g < 7 else 2):
                    whi(N_PLE + 4 * g + 2 + j, (2 + j) % 4)
                if g == 0:
                    root(4, 6, 1, D)
                    root(5, 7, 2, D)
                act.wait_ge(emptied, G_PLE + g + 1)
                nc.scalar.activation(tmp[:, 0:2, :], tmp[:, 0:2, :], ACT.Sigmoid).then_inc(pg_sig, 1)
                for t in range(2):
                    square(72 + 2 * g + t, res[:, 2 * g + t, :], sq_b, pg_res, g + 1)
            root(6, 7, 0, D)

        @block.vector
        def _(dve):
            tt = nc.vector.tensor_tensor
            stt = nc.vector.scalar_tensor_tensor

            def wlo(n, j):
                dve.wait_ge(w_hi_done, n + 1)
                tt(w_lo[:, j % HL], raw[:, j], w_hi[:, j % HL], ALU.subtract).then_inc(w_lo_done, 1)

            def four(n):
                for j in range(4):
                    wlo(n + 2 + j, (2 + j) % 4)

            def both(r):
                return rstd[:, r:r + 1, :].broadcast_to([P, 2, SEQ])

            def empty(out, bank, r, n):
                dve.wait_ge(piece_used, n + 1)
                tt(out, ps[:, bank:bank + 2, :], both(r), ALU.mult).then_inc(emptied, 1)

            def recip(norm, r):
                dve.wait_ge(root_done, norm + 1)
                nc.vector.reciprocal(rstd[:, r, :], rstd[:, r, :]).then_inc(rstd_done, 1)
                dve.wait_ge(rstd_done, norm + 1)

            def gain_lo(out, in_, gain, n):
                dve.wait_ge(u_hi, n + 1)
                stt(out[:, 1, :], in_, gn[:, gain:gain + 1], out[:, 0, :], ALU.mult, ALU.subtract).then_inc(u_lo, 1)

            def head_norm(m, tile, gain):
                dve.wait_ge(hroot, m + 1)
                nc.vector.reciprocal(res[:, 14, :], res[:, 14, :]).then_inc(hrecip, 1)
                dve.wait_ge(hrecip, m + 1)
                stt(tile, tile, gn[:, gain:gain + 1], res[:, 14:15, :], ALU.mult, ALU.mult).then_inc(hnorm, 1)

            def rotate(m, tile, cs, tc, ts_, rows, before):
                if not isinstance(before, int) or before:
                    dve.wait_ge(op_hi, before)
                    dve.wait_ge(op_lo, before)
                tt(tc, tile, tab[0:rows, cs:cs + 1, :], ALU.mult).then_inc(by_cos, 1)
                dve.wait_ge(swapped, m + 1)
                tt(ts_, ps[0:rows, 7:8, :], tab[0:rows, cs + 1:cs + 2, :], ALU.mult).then_inc(by_sin, 1)
                dve.wait_ge(by_cos, m + 1)
                dve.wait_ge(by_sin, m + 1)
                tt(tc, tc, ts_, ALU.add).then_inc(roped, 1)

            def op_split(idx, out, in_, scale=None):
                dve.wait_ge(op_hi, idx + 1)
                if scale is None:
                    tt(out[:, 1, :], in_, out[:, 0, :], ALU.subtract).then_inc(op_lo, 1)
                else:
                    stt(out[:, 1, :], in_, scale, out[:, 0, :], ALU.mult, ALU.subtract).then_inc(op_lo, 1)

            SA, SB = float(HD) ** -0.5, float(QK_B) ** -0.5

            def softmax(n):
                for q in range(4):
                    dve.wait_ge(scores, n * 4 + q + 1)
                    nc.vector.tensor_reduce(negmax[:, q:q + 1], ps[:, 4 + q, :], AX_X, ALU.max,
                                            negate=True).then_inc(max_done, 1)
                for q in range(4):
                    dve.wait_ge(exp_done, n * 4 + q + 1)
                    nc.vector.reciprocal(rrow[:, q:q + 1], psumrow[:, q:q + 1]).then_inc(rsum_done, 1)
                    dve.wait_ge(rsum_done, n * 4 + q + 1)
                    nc.vector.tensor_scalar(res[:, PROB + q, :], res[:, PROB + q, :], rrow[:, q:q + 1], None,
                                            ALU.mult).then_inc(p_done, 1)

            def pt_split(n, kt, pt):
                dve.wait_ge(pt_hi, n * 4 + kt + 1)
                tt(pt[kt % 2][:, 1, :], ps[:, 4 + kt % 2, :], pt[kt % 2][:, 0, :], ALU.subtract).then_inc(pt_lo, 1)

            def o_split(n, out):
                dve.wait_ge(o_hi, n + 1)
                tt(out[:, :, 1, :], ps[:, 6:7, :], out[:, :, 0, :], ALU.subtract).then_inc(o_lo, 1)

            nc.vector.memset(eps[:], EPS).then_inc(set_done, 1)
            dve.wait_ge(const_in, 48)
            for k in range(KD):
                if k in (0, 4, 8, 12):
                    wlo(k // 4, k // 4)
                gain_lo(u_tile(k), res[:, k, :], G_MIX + k, k)
            wlo(4, 0)
            wlo(5, 1)
            recip(0, 0)
            dve.wait_ge(sq_done, 16)
            dve.wait_ge(u_lo, 16)
            for g, t0 in enumerate((8, 10, 0, 2, 4, 6)):
                if g:
                    four(4 * g)
                empty(res[:, t0:t0 + 2, :], 2 * (g % 2), 0, 4 * g + 3)
            dve.wait_ge(emptied, 6)
            for m, (t, gain) in enumerate(((8, G_KN), (9, G_KN), (0, G_QN))):
                head_norm(m, res[:, t:t + 1, :], gain)
                dve.wait_ge(hnorm, m + 1)
                rotate(m, res[:, t:t + 1, :], 0, res[:, 15:16, :], res[:, 14:15, :], P, m)
                dve.wait_ge(roped, m + 1)
                op_split(m, [K_A[0], K_A[1], Q_A][m], res[:, 15, :], SA if m == 2 else None)
                wlo(26 + m, (2 + m) % 4)
            for v in range(2):
                op_split(OP_V + v, V_A[v], ps[:, 4 + v, :])
            wlo(29, 1)
            dve.wait_ge(piece_used, 28)
            tt(res[:, 12, :], ps[:, 0, :], rstd[:, 0, :], ALU.mult).then_inc(emptied, 1)

            def gate_group(h, branch, n):
                if not isinstance(h, int) or h > 0:
                    dve.wait_ge(gate_out[branch], h * 16)
                empty(tmp[:, 2 * branch:2 * branch + 2, :], 2 - 2 * branch, 0, n)

            def gqa_head(h, kv, more):
                b = h * 8 + N_GATE
                tile = res[:, bass.ds(h + 1, 1), :] if more else None
                softmax(h)
                for j in range(4):
                    wlo(b + 2 + j, (2 + j) % 4)
                gate_group(h, 0, b + 3)
                pt_split(h, 0, PT_A)
                pt_split(h, 1, PT_A)
                wlo(b + 6, 2)
                pt_split(h, 2, PT_A)
                pt_split(h, 3, PT_A)
                wlo(b + 7, 3)
                o_split(h, r3[:, bass.ds(h, 1)])
                if more:
                    head_norm(h + 3, tile, G_QN)
                wlo(b + 8, 0)
                if more:
                    dve.wait_ge(hnorm, h + 4)
                    rotate(h + 3, tile, 0, res[:, 15:16, :], res[:, 14:15, :], P, h + 5)
                    dve.wait_ge(roped, h + 4)
                    op_split(h + 5, Q_A, res[:, 15, :], SA)
                wlo(b + 9, 1)
                gate_group(h, 1, b + 7)

            gqa_head(0, 0, True)
            with dve.Fori(1, GROUP) as h:
                gqa_head(h, 0, True)
            with dve.Fori(GROUP, HEADS - 1) as h:
                gqa_head(h, 1, True)
            gqa_head(HEADS - 1, 1, False)

            dve.wait_ge(gate_out[0], 16 * HEADS)
            for g in range(4):
                four(N_LAT + 4 * g)
                if g:
                    dve.wait_ge(u_hi, 16 + 2 * g)
                    dve.wait_ge(u_lo, 16 + 2 * g)
                    dve.wait_ge(sq_done, 16 + 2 * g)
                empty(tmp[:, 0:2, :], 2 * ((G_LAT + g) % 2), 0, N_LAT + 4 * g + 3)
                for t in range(2):
                    k = 2 * g + t
                    gain_lo(r2[:, k], tmp[:, t, :], G_QA + k, 16 + k)
            dve.wait_ge(emptied, G_GATE)
            kr = slice(0, ROPE_B)
            rotate(10, res[kr, 12:13, :], 2, res[kr, 6:7, :], res[kr, 7:8, :], ROPE_B, OP_KR)
            dve.wait_ge(roped, 11)
            op_split(OP_KR, KR_B[kr], res[kr, 6, :])

            def mla_q(h):
                dve.wait_ge(op_hi, h * 4 + OP_B)
                dve.wait_ge(op_lo, h * 4 + OP_B)
                empty(res[:, 0:2, :], 2, 1, h * 2 + N_B)

            def mla_kv(h):
                empty(res[:, 2:4, :], 0, 2, h * 2 + N_B + 1)

            def mla_rotate(h):
                dve.wait_ge(emptied, h * 2 + G_B + 2)
                rotate(h + 11, res[kr, 1:2, :], 2, res[kr, 6:7, :], res[kr, 7:8, :], ROPE_B, h * 4 + OP_B)
                dve.wait_ge(roped, h + 12)
                op_split(h * 4 + OP_B + 2, PE_B[kr], res[kr, 6, :], SB)

            recip(1, 1)
            mla_q(0)
            wlo(N_B + 2, 2)
            dve.wait_ge(emptied, G_B + 1)
            op_split(OP_B, Q_B, res[:, 0, :], SB)
            recip(2, 2)
            mla_kv(0)
            wlo(N_B + 3, 3)
            dve.wait_ge(emptied, G_B + 2)
            op_split(OP_B + 1, K_B, res[:, 2, :])
            mla_rotate(0)
            op_split(OP_B + 3, V_B, ps[:, 7, :])

            def mla_head(h, j0, more):
                n = h + HEADS
                b = h * 2 + N_B + 4
                softmax(n)
                if more:
                    mla_q(h + 1)
                    wlo(b, j0)
                    dve.wait_ge(emptied, h * 2 + G_B + 3)
                    op_split(h * 4 + OP_B + 4, Q_B, res[:, 0, :], SB)
                    mla_kv(h + 1)
                    wlo(b + 1, j0 + 1)
                    dve.wait_ge(emptied, h * 2 + G_B + 4)
                    op_split(h * 4 + OP_B + 5, K_B, res[:, 2, :])
                pt_split(n, 0, PT_B)
                pt_split(n, 1, PT_B)
                if more:
                    mla_rotate(h + 1)
                pt_split(n, 2, PT_B)
                pt_split(n, 3, PT_B)
                if more:
                    op_split(h * 4 + OP_B + 7, V_B, ps[:, 7, :])
                o_split(n, r0[:, bass.ds(h, 1)])

            with dve.Fori(0, HEADS // 2 - 1) as i:
                mla_head(i * 2, 0, True)
                mla_head(i * 2 + 1, 2, True)
            mla_head(HEADS - 2, 0, True)
            mla_head(HEADS - 1, 2, False)

            def gated(out, bank, gate, n):
                dve.wait_ge(piece_used, n + 1)
                tt(out, ps[:, bank:bank + 2, :], gate, ALU.mult).then_inc(emptied, 1)

            def merge(half, i, s):
                pair = i * 2 + half * 4 + s
                n = pair * 4 + N_MERGE
                wlo(n + 2, 2)
                wlo(n + 3, 3)
                dve.wait_ge(gate_in[s], i * 32 + half * 64 + 32)
                dve.wait_ge(w_lo_done, n + 4)
                gated(tmp[:, 0:2, :], 2, res[:, 8 + 4 * s:10 + 4 * s, :], n + 1)
                wlo(n + 4, 0)
                wlo(n + 5, 1)
                gated(tmp[:, 2:4, :], 0, res[:, 10 + 4 * s:12 + 4 * s, :], n + 3)
                r = r1 if half == 0 else r2
                out = r[:, bass.ds(i * 4 + 2 * s, 2)]
                dve.wait_ge(mrg_hi, pair + 1)
                tt(out[:, :, 1, :], tmp[:, 0:2, :], out[:, :, 0, :], ALU.subtract).then_inc(mrg_lo, 1)

            for half in range(2):
                with dve.Fori(0, 2) as i:
                    merge(half, i, 0)
                    merge(half, i, 1)

            def add_residual(d, pair, n):
                dve.wait_ge(piece_used, n + 1)
                r = res[:, 2 * d:2 * d + 2, :]
                tt(r, ps[:, 2 * pair:2 * pair + 2, :], r, ALU.add).then_inc(emptied, 1)

            for g in range(8):
                four(N_WO + 4 * g)
                dve.wait_ge(x_again[g // 4], 16)
                add_residual(g, (G_WO + g) % 2, N_WO + 4 * g + 3)
                dve.wait_ge(emptied, G_WO + g + 1)
                for k in (2 * g, 2 * g + 1):
                    gain_lo(n_tile(k), res[:, k, :], G_FFN + k, 24 + k)

            def ff_lo_part(e, half):
                dve.wait_ge(ff_hi, e + 1)
                tt(r1[:, 2 * half:2 * half + 2, 1, :], tmp[:, 2:4, :], r1[:, 2 * half:2 * half + 2, 0, :],
                   ALU.subtract).then_inc(ff_lo, 1)

            four(N_FF)
            recip(3, 0)
            empty(tmp[:, 0:2, :], 0, 0, N_FF + 3)
            dve.wait_ge(p_in, 16)
            for k in range(2):
                dve.wait_ge(u_hi, 41 + k)
                tt(P_T[k][:, 1, :], tab[:, 2 + k, :], P_T[k][:, 0, :], ALU.subtract).then_inc(u_lo, 1)

            def chunk(c, last):
                b, g = c * 24 + N_FF_LOOP, c * 12 + G_FF
                four(b)
                if not isinstance(c, int) or c > 0:
                    dve.wait_ge(ff_lo, c * 2)
                empty(tmp[:, 2:4, :], 2, 0, b + 3)
                wlo(b + 6, 2)
                ff_lo_part(c * 2, 0)
                for j in range(3):
                    wlo(b + 7 + j, (3 + j) % 4)
                dve.wait_ge(ff_mul, c * 2 + 1)
                empty(tmp[:, 0:2, :], 4, 0, b + 7)
                four(b + 8)
                dve.wait_ge(ff_lo, c * 2 + 1)
                empty(tmp[:, 2:4, :], 6, 0, b + 11)
                if not last:
                    wlo(b + 14, 2)
                    ff_lo_part(c * 2 + 1, 1)
                    for j in range(3):
                        wlo(b + 15 + j, (3 + j) % 4)
                    dve.wait_ge(ff_mul, c * 2 + 2)
                    empty(tmp[:, 0:2, :], 0, 0, b + 15)
                    dve.wait_ge(emptied, g + 1)
                    for d in range(8):
                        wlo(b + 18 + d, (2 + d) % 4)
                        add_residual(d, (1 + d) % 4, b + 16 + d)
                else:
                    for i in range(8):
                        wlo(b + 14 + i, (2 + i) % 4)
                        if i == 1:
                            ff_lo_part(c * 2 + 1, 1)
                        dve.wait_ge(piece_used, b + 12 + i + 1)
                        nc.vector.tensor_copy(emb[:, 2 * i:2 * i + 2, :],
                                              ps[:, 2 * (i % 4):2 * (i % 4) + 2, :]).then_inc(emptied, 1)

            chunk(0, False)
            with dve.Fori(1, CHUNKS - 1) as c:
                chunk(c, False)
            chunk(CHUNKS - 1, True)
            for d in range(8):
                wlo(N_D + 2 + d, (2 + d) % 4)
                add_residual(d, d % 4, N_D + d)
                dve.wait_ge(emptied, G_D + d + 1)
                for k in (2 * d, 2 * d + 1):
                    gain_lo(n_tile(k), res[:, k, :], G_PLEN + k, 42 + k)
            for g in range(8):
                for j in range(4 if g < 7 else 2):
                    wlo(N_PLE + 4 * g + 2 + j, (2 + j) % 4)
                if g == 0:
                    recip(4, 1)
                    recip(5, 2)
                for k in (2 * g, 2 * g + 1):
                    stt(emb[:, k, :], emb[:, k, :], gn[:, G_POST + k:G_POST + k + 1], rstd[:, 1, :],
                        ALU.mult, ALU.mult).then_inc(emb_normed, 1)
                if g:
                    dve.wait_ge(pg_res, g)
                empty(tmp[:, 0:2, :], 2 * (g % 4), 2, N_PLE + 4 * g + 3)
            recip(6, 0)
            dve.wait_ge(pg_res, 8)
            for k in range(KD):
                stt(res[:, k, :], res[:, k, :], gn[:, G_FIN + k:G_FIN + k + 1], rstd[:, 0, :],
                    ALU.mult, ALU.mult).then_inc(fin_done, 1)

        @block.gpsimd
        def _(pool):
            def add_square(s, first, norm, sq):
                out = sums(norm)
                pool.wait_ge(sq_done, s + 1)
                if s == first:
                    if norm == 4:
                        pool.wait_ge(u_lo, 42)
                    elif norm:
                        pool.wait_ge(tot_done, 4 if norm == 5 else norm)
                    nc.gpsimd.tensor_copy(out, sq[:, s % 2, :]).then_inc(acc_done, 1)
                else:
                    pool.wait_ge(acc_done, s)
                    nc.gpsimd.tensor_tensor(out, out, sq[:, s % 2, :], ALU.add).then_inc(acc_done, 1)

            sq_a, sq_b = tmp[:, 2:4, :], tab[:, 0:2, :]
            for norm, first, end in ((0, 0, 16), (1, 16, 20), (2, 20, 24)):
                for s in range(first, end):
                    add_square(s, first, norm, sq_a)

            with pool.Fori(0, 8) as i:
                pool.wait_ge(emptied, i * 2 + G_MERGE + 2)
                nc.gpsimd.tensor_tensor(tmp[:, 0:2, :], tmp[:, 0:2, :], tmp[:, 2:4, :], ALU.add).then_inc(mrg_sum, 1)
            for s in range(24, 40):
                add_square(s, 24, 3, sq_b)
            with pool.Fori(0, CHUNKS) as c:
                for half in range(2):
                    pool.wait_ge(emptied, c * 12 + G_FF + 2 + 2 * half)
                    pool.wait_ge(ff_act, c * 2 + half + 1)
                    nc.gpsimd.tensor_tensor(tmp[:, 2:4, :], tmp[:, 2:4, :], tmp[:, 0:2, :],
                                            ALU.mult).then_inc(ff_mul, 1)
            for norm, first in ((4, 40), (5, 56)):
                for s in range(first, first + 16):
                    add_square(s, first, norm, sq_b)
            for g in range(8):
                pool.wait_ge(pg_sig, g + 1)
                pool.wait_ge(emb_normed, 2 * g + 2)
                nc.gpsimd.tensor_tensor(tmp[:, 0:2, :], tmp[:, 0:2, :], emb[:, 2 * g:2 * g + 2, :],
                                        ALU.mult).then_inc(pg_mul, 1)
                pool.wait_ge(pg_mul, g + 1)
                pool.wait_ge(u_hi, 58)
                pool.wait_ge(u_lo, 58)
                pool.wait_ge(sq_done, 72 + 2 * g)
                r = res[:, 2 * g:2 * g + 2, :]
                nc.gpsimd.tensor_tensor(r, r, tmp[:, 0:2, :], ALU.add).then_inc(pg_res, 1)
                for s in (72 + 2 * g, 73 + 2 * g):
                    add_square(s, 72, 6, sq_b)


INPUTS = ["xT", "pT", "gains", "tables", "mats", "w_in", "w_qb", "w_kvb", "w_a", "w_b", "w_o", "w_gu", "w_dn",
          "w_pg", "w_pp"]


def rotary_tables():
    s = np.arange(SEQ)
    out = np.zeros((P, 4, SEQ), np.float32)
    for i, d in enumerate((HD, ROPE_B)):
        half, n2 = d // 2, d // 4
        inv = (1.0 / (np.float32(THETA) ** (np.arange(0, half, 2, dtype=np.float32) / np.float32(half)))
               ).astype(np.float32)
        for f in range(d):
            pos = (s // GRID_W if f < half else s % GRID_W).astype(np.float32)
            ang = pos * inv[f % n2]
            out[f, 2 * i] = np.cos(ang)
            out[f, 2 * i + 1] = np.sin(ang) * np.float32(-1.0 if f % half < n2 else 1.0)
    return out


def matrices():
    out = np.zeros((P, 4, P), np.float32)
    i = np.arange(P)
    out[i, 0, i] = 1.0
    out[:, 1, :] = 1.0
    out[i, 2, i ^ (HD // 4)] = 1.0
    out[i, 3, i ^ (ROPE_B // 4)] = 1.0
    return out


def kernel(**inputs):
    import concourse.bacc as _bacc
    from concourse.bass_utils import run_bass_kernel_spmd as _run

    a = {k: np.asarray(v) for k, v in inputs.items()}
    tiles = ("g_mix", "g_ffn", "g_ple", "g_ple_post", "g_final", "q_a_norm", "kv_a_norm", "q_norm_a", "k_norm_a")
    given = {
        "xT": a["x"][0].T, "pT": a["p"][0, 0].T,
        "gains": np.concatenate([a[k].reshape(-1, P).T for k in tiles], axis=1),
        "tables": rotary_tables(), "mats": matrices(),
        "w_in": a["w_in"][0], "w_qb": a["w_q_b"][0], "w_kvb": a["w_kv_b"][0], "w_a": a["w_a_out"][0],
        "w_b": a["w_b_out"][0], "w_o": a["w_o"][0], "w_gu": a["w_gate_up"][0], "w_dn": a["w_down"][0],
        "w_pg": a["w_ple_gate"][0], "w_pp": a["w_ple_proj"][0],
    }
    given = {k: np.ascontiguousarray(v) for k, v in given.items()}
    nc = _bacc.Bacc("TRN2", target_bir_lowering=False, num_devices=1, dynamic_dma_scratch_size=1024)
    args = [nc.dram_tensor(k, given[k].shape, F32, kind="ExternalInput").ap() for k in INPUTS]
    out = nc.dram_tensor("outT", (D, SEQ), F32, kind="ExternalOutput").ap()
    build(nc, *args, out)
    r = _run(nc, [{k: given[k] for k in INPUTS}], core_ids=[0])
    return np.ascontiguousarray(r.results[0]["outT"].T)[None]
```

```python
from contextlib import ExitStack

import numpy as np

import concourse.bass as bass
from concourse import mybir

F32 = mybir.dt.float32
F32R = mybir.dt.float32r
ALU = mybir.AluOpType
ACT = mybir.ActivationFunctionType
AX_X = mybir.AxisListType.X

P = 128
SEQ = 512
D = 2048
KD = D // P
HEADS, KV_HEADS, HD = 8, 2, 128
GROUP = HEADS // KV_HEADS
LORA = 512
KL = LORA // P
ROPE_B = 64
QK_B = 128 + ROPE_B
D_FF = 5632
CHUNKS = D_FF // 512
PLE = 256
EPS = 1e-6
GRID_W = 64
THETA = 10000.0
COLS = 256
KP = 4
RAW = 4
HL = 2

C_Q, C_K, C_V = 0, 1024, 1280
C_CQ, C_CKV, C_KR = 1536, 2048, 2560
C_GA, C_GB = 2624, 4672

N_QKV, N_GATE = 0, 28
N_LAT = N_GATE + 8 * 8
N_B = N_LAT + 16
N_MERGE = N_B + 16
N_WO = N_MERGE + 32
N_FF = N_WO + 32
N_FF_LOOP = N_FF + 4
N_FF_LAST = N_FF_LOOP + 24 * (CHUNKS - 1)
N_E = N_FF_LAST + 12
N_D = N_E + 4
N_PLE = N_D + 8
N_END = N_PLE + 32
G_GATE = 7
G_LAT = G_GATE + 16
G_B = G_LAT + 4
G_MERGE = G_B + 16
G_WO = G_MERGE + 16
G_FF = G_WO + 8
G_FF_LOOP = G_FF + 1
G_FF_LAST = G_FF_LOOP + 12 * (CHUNKS - 1)
G_E = G_FF_LAST + 3
G_D = G_E + 8
G_PLE = G_D + 8
G_END = G_PLE + 8

G_MIX, G_FFN, G_PLEN, G_POST, G_FIN, G_QA, G_KVA, G_QN, G_KN = 0, 16, 32, 48, 64, 80, 84, 88, 89
GAINS = 90

OP_Q, OP_KR, OP_B = 4, 12, 13


def build(nc, xT, pT, gains, tables, mats, w_in, w_qb, w_kvb, w_a, w_b, w_o, w_gu, w_dn, w_pg, w_pp, outT):
    with ExitStack() as ctx:
        def sb(name, shape, dt=F32):
            return ctx.enter_context(nc.sbuf_tensor(name, shape, dt))

        def sem(name):
            return ctx.enter_context(nc.semaphore(name))

        raw = sb("raw", [P, RAW, KP, COLS])
        w_hi = sb("w_hi", [P, HL, KP, COLS], F32R)
        w_lo = sb("w_lo", [P, HL, KP, COLS], F32R)
        res = sb("res", [P, KD, SEQ])
        tmp = sb("tmp", [P, 4, SEQ])
        tab = sb("tab", [P, 4, SEQ])
        acc = sb("acc", [P, SEQ])
        rstd = sb("rstd", [P, 3, SEQ])
        cm = sb("cm", [P, 4, P])
        gn = sb("gn", [P, GAINS])
        eps = sb("eps", [P, 1])
        negmax = sb("negmax", [P, 4])
        psumrow = sb("psumrow", [P, 4])
        rrow = sb("rrow", [P, 4])
        r0 = sb("r0", [P, 8, 2, SEQ], F32R)
        r1 = sb("r1", [P, 8, 2, SEQ], F32R)
        r3 = sb("r3", [P, 8, 2, SEQ], F32R)
        with nc.sbuf_tensor("r2", [P, 8, 2, SEQ], F32R) as r2:
            pass
        emb = sb("emb", [P, KD, SEQ])
        ident, ones, swap_a, swap_b = (cm[:, i, :] for i in range(4))
        ps = ctx.enter_context(nc.psum_tensor("ps", [P, 8, SEQ], F32))
        gates = nc.dram_tensor("gates", [2, KD, P, SEQ], F32, kind="Internal").ap()

        raw_in = [sem(f"raw_in{i}") for i in range(RAW)]
        w_hi_done, w_lo_done, piece_used = sem("w_hi_done"), sem("w_lo_done"), sem("piece_used")
        emptied = sem("emptied")
        x_in = [sem(f"x_in{i}") for i in range(4)]
        x_first = sem("x_first")
        x_again = [sem(f"x_again{i}") for i in range(2)]
        gains_in, mats_in, tables_in, p_in = sem("gains_in"), sem("mats_in"), sem("tables_in"), sem("p_in")
        gate_in = [sem(f"gate_in{i}") for i in range(2)]
        gate_out = [sem(f"gate_out{i}") for i in range(2)]
        u_hi, u_lo = sem("u_hi"), sem("u_lo")
        sq_done, acc_done, tot_done = sem("sq_done"), sem("acc_done"), sem("tot_done")
        log_done, root_done, refine, rstd_done = sem("log_done"), sem("root_done"), sem("refine"), sem("rstd_done")
        hsq, htot, hlog, hroot = sem("hsq"), sem("htot"), sem("hlog"), sem("hroot")
        hrefine, hnorm = sem("hrefine"), sem("hnorm")
        swapped, by_cos, by_sin, roped = sem("swapped"), sem("by_cos"), sem("by_sin"), sem("roped")
        v_turned, op_hi, op_lo = sem("v_turned"), sem("op_hi"), sem("op_lo")
        scores, max_done, exp_done, rsum_done, p_done = (sem("scores"), sem("max_done"), sem("exp_done"),
                                                         sem("rsum_done"), sem("p_done"))
        p_turned, pt_hi, pt_lo, pv_done = sem("p_turned"), sem("pt_hi"), sem("pt_lo"), sem("pv_done")
        o_hi, o_lo = sem("o_hi"), sem("o_lo")
        gate_sig = sem("gate_sig")
        mrg_sum, mrg_hi, mrg_lo = sem("mrg_sum"), sem("mrg_hi"), sem("mrg_lo")
        ff_act, ff_mul, ff_hi, ff_lo = sem("ff_act"), sem("ff_mul"), sem("ff_hi"), sem("ff_lo")
        emb_group, emb_normed = sem("emb_group"), sem("emb_normed")
        tail_tile, tail_emptied, tail_mul, tail_res = (sem("tail_tile"), sem("tail_emptied"), sem("tail_mul"),
                                                       sem("tail_res"))
        pg_sig, pg_mul, pg_res, gained = sem("pg_sig"), sem("pg_mul"), sem("pg_res"), sem("gained")
        fin_dve, fin_pool, out_done = sem("fin_dve"), sem("fin_pool"), sem("out_done")
        set_done = sem("set_done")

        def u_tile(k):
            return (r0 if k < 8 else r1)[:, k % 8]

        def m_tile(k):
            return (r1 if k < 8 else r2)[:, k % 8]

        def as_2_by_512(slot):
            return slot.rearrange("p k c -> p (k c)").rearrange("p (k c) -> p k c", k=2)

        def sums(norm):
            return tab[:, 3, :] if norm == 4 else acc[:]

        def ff_pair(g):
            return (g - G_FF + 2) % 4

        def n_tile(k):
            return (r3 if k < 8 else r0)[:, k % 8]

        K_A, V_A, Q_A = [r2[:, 0], r2[:, 1]], [r2[:, 2], r2[:, 3]], r2[:, 4]
        PT_A = [r2[:, 5], r2[:, 6], r2[:, 7]]
        Q_B, PE_B, K_B, V_B, KR_B = (r1[:, i] for i in range(5))
        PT_B = [r1[:, 5], r1[:, 6], r1[:, 7]]
        PT_BANK = [4, 5, 7, 4]
        P_T = [r1[:, 4], r1[:, 5]]
        PROB = 8
        GATE_IN = [12, 8]

        TAIL_BANK = 2 * ((ff_pair(G_PLE + 7) + 3) % 4)
        FIN_POOL = 6
        FIN_ORDER = [6, 8, 0, 10, 2, 12, 14, 4]

        block = ctx.enter_context(nc.Block())

        @block.sync
        def _(sp):
            def load(n, j, w, k0, col, cols=COLS):
                src = w[k0 * P:(k0 + KP) * P, :].rearrange("(k p) c -> p k c", p=P)[:, :, bass.ds(col, cols)]
                if not isinstance(n, int) or n >= RAW:
                    sp.wait_ge(w_lo_done, n - RAW + 1)
                sp.dma_start(raw[:, j, :, 0:cols], src).then_inc(raw_in[j], 16)

            x_v = xT.rearrange("(k p) s -> p k s", p=P)
            load(0, 0, w_in, 0, C_K)
            sp.dma_start(res[:, 0:2, :], x_v[:, 0:2, :]).then_inc(x_first, 16)
            sp.dma_start(res[:, 2:4, :], x_v[:, 2:4, :]).then_inc(x_in[0], 16)
            load(1, 1, w_in, 4, C_K)
            sp.dma_start(res[:, 4:8, :], x_v[:, 4:8, :]).then_inc(x_in[1], 16)
            load(2, 2, w_in, 8, C_K)
            sp.dma_start(res[:, 8:12, :], x_v[:, 8:12, :]).then_inc(x_in[2], 16)
            load(3, 3, w_in, 12, C_K)
            sp.dma_start(res[:, 12:16, :], x_v[:, 12:16, :]).then_inc(x_in[3], 16)
            sp.dma_start(cm[:], mats).then_inc(mats_in, 16)
            n = 4
            for col in [C_V, C_KR, C_Q, C_Q + 256, C_Q + 512, C_Q + 768]:
                for j in range(4):
                    load(n + j, j, w_in, 4 * j, col)
                if n == 4:
                    sp.dma_start(tab[:], tables).then_inc(tables_in, 16)
                n += 4
            with sp.Fori(0, HEADS) as h:
                ca, cb = sp.snap(h * COLS + C_GA), sp.snap(h * COLS + C_GB)
                for j in range(8):
                    load(h * 8 + N_GATE + j, j % 4, w_in, 4 * (j % 4), ca if j < 4 else cb)
            for g in range(4):
                for j in range(4):
                    load(N_LAT + 4 * g + j, j, w_in, 4 * j, C_CQ + COLS * g)
            with sp.Fori(0, HEADS // 2) as i:
                for s in range(2):
                    cq, ckv = sp.snap(i * (2 * QK_B) + s * QK_B), sp.snap(i * (2 * COLS) + s * COLS)
                    load(i * 4 + N_B + 2 * s, 2 * s, w_qb, 0, cq, cols=QK_B)
                    load(i * 4 + N_B + 2 * s + 1, 2 * s + 1, w_kvb, 0, ckv)
            x_tiles = xT.rearrange("(k p) s -> p k s", p=P)
            with sp.Fori(0, 4) as i:
                for s in range(2):
                    col = sp.snap(i * (2 * COLS) + s * COLS)
                    t = sp.snap(i * 4 + 2 * s)
                    for b, w in enumerate((w_a, w_b)):
                        for j in range(2):
                            load(i * 8 + N_MERGE + 4 * s + 2 * b + j, 2 * b + j, w, 4 * j, col)
                    sp.wait_ge(gate_out[0], 16 * HEADS)
                    sp.wait_ge(gate_out[1], 16 * HEADS)
                    if s == 1:
                        sp.wait_ge(p_turned, 8 * HEADS)
                    sp.wait_ge(emptied, i * 4 + 2 * s + G_MERGE - 2)
                    for b in range(2):
                        sp.dma_start(res[:, GATE_IN[s] + 2 * b:GATE_IN[s] + 2 * b + 2, :],
                                     gates[b].rearrange("k p s -> p k s")[:, bass.ds(t, 2), :]
                                     ).then_inc(gate_in[s], 16)
            sp.wait_ge(op_lo, OP_B + 4 * HEADS)
            sp.dma_start(res[:, 0:8, :], x_tiles[:, 0:8, :]).then_inc(x_again[0], 16)
            for j in range(4):
                load(N_WO + j, j, w_o, 4 * j, 0)
            sp.wait_ge(emptied, G_WO)
            sp.dma_start(res[:, 8:16, :], x_tiles[:, 8:16, :]).then_inc(x_again[1], 16)
            with sp.Fori(1, 8) as g:
                col = sp.snap(g * COLS)
                for j in range(4):
                    load(g * 4 + N_WO + j, j, w_o, 4 * j, col)

            def group4(n, w, col):
                for j in range(4):
                    load(n + j, j, w, 4 * j, col)

            def down_rows(n, row):
                for d in range(8):
                    src = w_dn[bass.ds(row, 512), d * COLS:(d + 1) * COLS].rearrange("(k p) c -> p k c", p=P)
                    sp.wait_ge(w_lo_done, n + d - RAW + 1)
                    sp.dma_start(raw[:, d % 4], src).then_inc(raw_in[d % 4], 16)

            sp.dma_start(tab[:, 2:4, :], pT.rearrange("(k p) s -> p k s", p=P)).then_inc(p_in, 16)
            group4(N_FF, w_gu, 0)
            with sp.Fori(0, CHUNKS - 1) as c:
                cols = [sp.snap(c * 512 + off) for off in (D_FF, 256, D_FF + 256, 512)]
                row = sp.snap(c * 512)
                for g in range(4):
                    group4(c * 24 + N_FF_LOOP + 4 * g, w_gu, cols[g])
                down_rows(c * 24 + N_FF_LOOP + 16, row)
            last = 512 * (CHUNKS - 1)
            for g, off in enumerate((D_FF, 256, D_FF + 256)):
                group4(N_FF_LAST + 4 * g, w_gu, last + off)
            for g in range(4):
                src = w_pp[:, 512 * g:512 * g + 512].rearrange("(k p) c -> p k c", p=P)
                sp.wait_ge(w_lo_done, N_E + g - RAW + 1)
                sp.dma_start(as_2_by_512(raw[:, g]), src).then_inc(raw_in[g], 16)
            down_rows(N_D, last)
            with sp.Fori(0, 8) as g:
                col = sp.snap(g * COLS)
                for j in range(4):
                    load(g * 4 + N_PLE + j, j, w_pg, 4 * j, col)
            o_v = outT.rearrange("(k p) s -> p k s", p=P)
            for i, t in enumerate(FIN_ORDER):
                if t < FIN_POOL:
                    sp.wait_ge(fin_pool, t // 2 + 1)
                else:
                    sp.wait_ge(fin_dve, (t - FIN_POOL) // 2 + 1)
                sp.dma_start(o_v[:, t:t + 2, :], emb[:, t:t + 2, :]).then_inc(out_done, 16)
            sp.wait_ge(out_done, 16 * KD // 2)

        @block.tensor
        def _(pe):
            mm = nc.tensor.matmul

            def product(out, hi, lo, x, start, stop):
                mm(out, hi, x[:, 0, :], start=start, stop=False)
                mm(out, hi, x[:, 1, :], start=False, stop=False)
                return mm(out, lo, x[:, 0, :], start=False, stop=stop)

            def piece(n, j, bank, xs, first, last, tiles=2, before=None):
                pe.wait_ge(w_lo_done, n + 1)
                s = j % HL
                for k, x in enumerate(xs):
                    if before:
                        before(k)
                    for t in range(tiles):
                        i = product(ps[:, bank + t, :], w_hi[:, s, k, P * t:P * t + P], w_lo[:, s, k, P * t:P * t + P],
                                    x, first and k == 0, last and k == len(xs) - 1)
                i.then_inc(piece_used, 1)

            def free(g, lag=2):
                if not isinstance(g, int) or g >= lag:
                    pe.wait_ge(emptied, g - lag + 1)

            def total(norm, bank):
                pe.wait_ge(acc_done, [16, 20, 24, 40, 56, 72][norm])
                mm(ps[:, bank, :], ones, sums(norm), start=True, stop=True).then_inc(tot_done, 1)

            def head_total(m):
                pe.wait_ge(hsq, m + 1)
                mm(ps[:, 7:8, :], ones, res[:, 13:14, :], start=True, stop=True).then_inc(htot, 1)

            def head_swap(m, tile):
                pe.wait_ge(hnorm, m + 1)
                mm(ps[:, 7:8, :], swap_a, tile, start=True, stop=True).then_inc(swapped, 1)

            def turn_v(tile, bank):
                for kt in range(4):
                    i = nc.tensor.transpose(ps[:, bank, kt * P:(kt + 1) * P], tile[:, kt * P:(kt + 1) * P], ident)
                i.then_inc(v_turned, 1)

            def score(n, q_ops, k_ops, need):
                def part(q, qo, ko, start, stop):
                    return product(ps[:, 4 + q, :], qo[:, 0, q * P:(q + 1) * P], qo[:, 1, q * P:(q + 1) * P],
                                   ko, start, stop)

                pe.wait_ge(op_lo, need)
                for q in (range(4) if len(q_ops) == 1 else (0, 1, 3, 2)):
                    if q == 2 and not (isinstance(n, int) and n == 0):
                        pe.wait_ge(o_lo, n)
                    i = part(q, q_ops[0], k_ops[0], True, len(q_ops) == 1)
                    if len(q_ops) == 1:
                        i.then_inc(scores, 1)
                if len(q_ops) == 2:
                    pe.wait_ge(op_lo, need + 1)
                    for q in range(4):
                        part(q, q_ops[1], k_ops[1], False, True).then_inc(scores, 1)

            def turn_p(n, kt):
                if kt == 0:
                    pe.wait_ge(p_done, n * 4 + 4)
                if kt == 3:
                    pe.wait_ge(pt_lo, n * 4 + 1)
                for q in range(4):
                    i = nc.tensor.transpose(ps[:, PT_BANK[kt], q * P:(q + 1) * P],
                                            res[:, PROB + q, kt * P:(kt + 1) * P], ident)
                i.then_inc(p_turned, 1)

            def weigh(n, kt, v, pt):
                pe.wait_ge(pt_lo, n * 4 + kt + 1)
                product(ps[:, 6, :], v[:, 0, kt * P:(kt + 1) * P], v[:, 1, kt * P:(kt + 1) * P], pt[kt % 3],
                        kt == 0, kt == 3).then_inc(pv_done, 1)

            def u_pieces(j):
                return [u_tile(4 * j + k) for k in range(4)]

            def in_group(g, after=None, tiles=2):
                free(g)
                for j in range(4):
                    def tile_ready(k, j=j):
                        pe.wait_ge(u_lo, 4 * j + k + 1)

                    piece(4 * g + j, j, 2 * (g % 2), u_pieces(j), j == 0, j == 3, tiles,
                          tile_ready if g == 0 else None)
                    for step in (after or {}).get(j, []):
                        step()

            in_group(0)

            def first_total():
                pe.wait_ge(mats_in, 16)
                total(0, 7)

            in_group(1, {1: [first_total]})
            in_group(2, tiles=1)
            in_group(3)
            k0, k1, q0 = res[:, 8:9, :], res[:, 9:10, :], res[:, 0:1, :]
            pe.wait_ge(rstd_done, 1)
            in_group(4, {0: [lambda: head_total(0)], 2: [lambda: head_swap(0, k0)],
                         3: [lambda: turn_v(res[:, 10, :], 4)]})

            def next_total(m):
                pe.wait_ge(by_sin, m)
                head_total(m)

            in_group(5, {0: [lambda: next_total(1)], 2: [lambda: head_swap(1, k1)],
                         3: [lambda: turn_v(res[:, 11, :], 5)]})
            in_group(6, {0: [lambda: next_total(2)], 2: [lambda: head_swap(2, q0)]})

            def gqa_head(h, kv, more):
                b = h * 8 + N_GATE
                score(h, [Q_A], [K_A[kv]], h + 5)
                free(h * 2 + G_GATE)
                piece(b, 0, 2, u_pieces(0), True, False)
                piece(b + 1, 1, 2, u_pieces(1), False, False)
                if more:
                    pe.wait_ge(exp_done, h * 4 + 4)
                    head_total(h + 3)
                piece(b + 2, 2, 2, u_pieces(2), False, False)
                piece(b + 3, 3, 2, u_pieces(3), False, True)
                if more:
                    head_swap(h + 3, res[:, bass.ds(h + 1, 1), :])
                turn_p(h, 0)
                turn_p(h, 1)
                free(h * 2 + G_GATE + 1)
                piece(b + 4, 4, 0, u_pieces(0), True, False)
                weigh(h, 0, V_A[kv], PT_A)
                if more:
                    pe.wait_ge(by_sin, h + 4)
                turn_p(h, 2)
                turn_p(h, 3)
                piece(b + 5, 5, 0, u_pieces(1), False, False)
                weigh(h, 1, V_A[kv], PT_A)
                weigh(h, 2, V_A[kv], PT_A)
                weigh(h, 3, V_A[kv], PT_A)
                piece(b + 6, 6, 0, u_pieces(2), False, False)
                piece(b + 7, 7, 0, u_pieces(3), False, True)

            gqa_head(0, 0, True)
            with pe.Fori(1, GROUP) as h:
                gqa_head(h, 0, True)
            with pe.Fori(GROUP, HEADS - 1) as h:
                gqa_head(h, 1, True)
            gqa_head(HEADS - 1, 1, False)

            def pe_swap(m, src, bank):
                mm(ps[:, bank, :], swap_b[0:ROPE_B, :], src, start=True, stop=True).then_inc(swapped, 1)

            for g in range(4):
                free(G_LAT + g)
                for j in range(4):
                    piece(N_LAT + 4 * g + j, j, 2 * ((G_LAT + g) % 2), u_pieces(j), j == 0, j == 3)
                if g == 0:
                    pe_swap(10, res[0:ROPE_B, 12, :], 7)
                if g == 2:
                    total(1, 6)

            def mla_q(h):
                free(h * 2 + G_B)
                piece(h * 2 + N_B, 0, 2, [r2[:, k] for k in range(4)], True, True)

            def mla_kv(h, before=None):
                free(h * 2 + G_B + 1)
                piece(h * 2 + N_B + 1, 1, 0, [r2[:, 4 + k] for k in range(4)], True, True, before=before)

            def mla_swap(h):
                pe.wait_ge(emptied, h * 2 + G_B + 1)
                pe_swap(h + 11, res[0:ROPE_B, 1, :], 2)

            def mla_turn_v(h):
                pe.wait_ge(emptied, h * 2 + G_B + 2)
                turn_v(res[:, 3, :], 0)

            pe.wait_ge(u_lo, 20)
            mla_q(0)

            def first_kv(k):
                pe.wait_ge(u_lo, 21 + k)
                if k == 2:
                    pe.wait_ge(by_sin, 11)
                    total(2, 7)
                    mla_swap(0)

            mla_kv(0, first_kv)
            mla_turn_v(0)
            pe.wait_ge(rstd_done, 3)
            PE_B_64, KR_B_64 = PE_B[0:ROPE_B], KR_B[0:ROPE_B]

            def mla_head(h, between):
                n = h + HEADS
                score(n, [Q_B, PE_B_64], [K_B, KR_B_64], h * 4 + OP_B + 2)
                between()
                turn_p(n, 0)
                turn_p(n, 1)
                turn_p(n, 2)

            def mla_head_more(h):
                n = h + HEADS

                def up():
                    pe.wait_ge(by_sin, h + 12)
                    mla_q(h + 1)
                    pe.wait_ge(op_lo, h * 4 + OP_B + 4)
                    mla_kv(h + 1)

                mla_head(h, up)
                mla_swap(h + 1)
                turn_p(n, 3)
                weigh(n, 0, V_B, PT_B)
                mla_turn_v(h + 1)
                for kt in (1, 2, 3):
                    weigh(n, kt, V_B, PT_B)

            with pe.Fori(0, HEADS - 1) as h:
                mla_head_more(h)

            def merge_group(pair, b, outputs_ready=None):
                free(pair * 2 + G_MERGE + b)
                r = (r3, r0)[b]
                for j in range(2):
                    if outputs_ready:
                        outputs_ready(j)
                    piece(pair * 4 + N_MERGE + 2 * b + j, j, 2 * (1 - b), [r[:, 4 * j + k] for k in range(4)],
                          j == 0, j == 1)

            def first_a():
                pe.wait_ge(o_lo, HEADS)
                pe.wait_ge(by_sin, 19)
                merge_group(0, 0)

            mla_head(HEADS - 1, first_a)
            turn_p(15, 3)
            for kt in range(4):
                weigh(15, kt, V_B, PT_B)

            def outputs_ready(j):
                pe.wait_ge(o_lo, HEADS + 4 * j + 4)

            merge_group(0, 1, outputs_ready)
            merge_group(1, 0)
            merge_group(1, 1)
            merge_group(2, 0)
            with pe.Fori(1, 3) as i:
                for s in range(2):
                    merge_group(i * 2 + s, 1)
                    merge_group(i * 2 + s + 1, 0)
            merge_group(6, 1)
            merge_group(7, 0)
            merge_group(7, 1)

            with pe.Fori(0, 4) as i:
                for s in range(2):
                    free(i * 2 + G_WO + s)
                    for j in range(4):
                        pe.wait_ge(mrg_lo, 2 * j + 2)
                        piece(i * 8 + N_WO + 4 * s + j, j, 2 * (1 - s), [m_tile(4 * j + k) for k in range(4)],
                              j == 0, j == 3)

            def n_group(g, n, pair):
                free(g, 4)
                for j in range(4):
                    piece(n + j, j, 2 * pair, [n_tile(4 * j + k) for k in range(4)], j == 0, j == 3)

            def down(g, n, pair0, need):
                pe.wait_ge(ff_lo, need)
                for d in range(8):
                    free(g + d, 4)
                    piece(n + d, d, 2 * ((pair0 + d) % 4), [r1[:, k] for k in range(4)], True, True)

            pe.wait_ge(op_lo, OP_B + 4 * HEADS)
            for j in range(4):
                pe.wait_ge(u_lo, 24 + 4 * j + 4)
                piece(N_FF + j, j, 4, [n_tile(4 * j + k) for k in range(4)], j == 0, j == 3)
            pe.wait_ge(emptied, G_FF)
            total(3, 3)
            n_group(G_FF + 1, N_FF_LOOP, 3)
            n_group(G_FF + 2, N_FF_LOOP + 4, 0)
            pe.wait_ge(rstd_done, 4)
            n_group(G_FF + 3, N_FF_LOOP + 8, 1)

            def next_and_down(c):
                n_group(c * 12 + G_FF + 4, c * 24 + N_FF_LOOP + 12, 2)
                down(c * 12 + G_FF + 5, c * 24 + N_FF_LOOP + 16, 3, c * 2 + 2)
                n_group(c * 12 + G_FF + 13, c * 24 + N_FF_LOOP + 24, 3)
                n_group(c * 12 + G_FF + 14, c * 24 + N_FF_LOOP + 28, 0)
                n_group(c * 12 + G_FF + 15, c * 24 + N_FF_LOOP + 32, 1)

            with pe.Fori(0, CHUNKS - 1) as c:
                next_and_down(c)
            pe.wait_ge(u_lo, 42)
            for g in range(8):
                free(G_E + g, 4)
                n, s = N_E + g // 2, (N_E + g // 2) % HL
                pe.wait_ge(w_lo_done, n + 1)
                hi, lo = as_2_by_512(w_hi[:, s]), as_2_by_512(w_lo[:, s])
                for t in range(2):
                    c = 256 * (g % 2) + P * t
                    for k in range(2):
                        i = product(ps[:, 2 * ff_pair(G_E + g) + t, :], hi[:, k, c:c + P], lo[:, k, c:c + P], P_T[k],
                                    k == 0, k == 1)
                i.then_inc(piece_used if g % 2 else emb_group, 1)
            down(G_D, N_D, ff_pair(G_D), 2 * CHUNKS)
            free(G_PLE, 4)
            for j in range(4):
                pe.wait_ge(u_lo, 42 + 4 * j + 4)
                piece(N_PLE + j, j, 2 * ff_pair(G_PLE), [n_tile(4 * j + k) for k in range(4)], j == 0, j == 3)
            pe.wait_ge(emptied, G_PLE)
            total(5, 3)
            total(4, 2)
            n_group(G_PLE + 1, N_PLE + 4, ff_pair(G_PLE + 1))
            n_group(G_PLE + 2, N_PLE + 8, ff_pair(G_PLE + 2))
            pe.wait_ge(rstd_done, 6)
            n_group(G_PLE + 3, N_PLE + 12, ff_pair(G_PLE + 3))
            for g in range(4, 7):
                n_group(G_PLE + g, N_PLE + 4 * g, ff_pair(G_PLE + g))
            free(G_PLE + 7, 4)
            n, bank = N_PLE + 28, 2 * ff_pair(G_PLE + 7)
            for j in range(3):
                piece(n + j, j, bank, [n_tile(4 * j + k) for k in range(4)], j == 0, False)
            pe.wait_ge(w_lo_done, n + 4)
            for t in range(2):
                for k in range(4):
                    i = product(ps[:, bank + t, :], w_hi[:, 1, k, P * t:P * t + P], w_lo[:, 1, k, P * t:P * t + P],
                                n_tile(12 + k), False, k == 3)
                i.then_inc(tail_tile, 1)
            pe.wait_ge(emptied, G_PLE + 7)
            pe.wait_ge(acc_done, 87)
            mm(ps[:, TAIL_BANK, :], ones, sums(6), start=True, stop=False)
            pe.wait_ge(sq_done, 88)
            mm(ps[:, TAIL_BANK, :], ones, tab[:, 1, :], start=False, stop=True).then_inc(tot_done, 1)

        @block.scalar
        def _(act):
            def copy(out, in_, scale=1.0):
                return nc.scalar.activation(out, in_, ACT.Copy, scale=scale)

            def whi(n, j):
                count = (n - j) * 4 + 16
                act.wait_ge(raw_in[j], count)
                if not isinstance(n, int) or n >= HL:
                    act.wait_ge(piece_used, n - HL + 1)
                copy(w_hi[:, j % HL], raw[:, j]).then_inc(w_hi_done, 1)

            def square(s, tile, sq, need, count):
                act.wait_ge(need, count)
                if s >= 2:
                    act.wait_ge(acc_done, s - 1)
                nc.scalar.activation(sq[:, s % 2, :], tile, ACT.Square).then_inc(sq_done, 1)

            def root(turn, bank, dst, width):
                act.wait_ge(tot_done, turn + 1)
                nc.scalar.activation(rstd[:, dst, :], ps[:, bank, :], ACT.Ln, scale=1.0 / width,
                                     bias=eps[:]).then_inc(log_done, 1)
                act.wait_ge(log_done, turn + 1)
                nc.scalar.activation(rstd[:, dst, :], rstd[:, dst, :], ACT.Exp, scale=-0.5).then_inc(root_done, 1)

            sq_a = tmp[:, 2:4, :]
            sq_b = tab[:, 0:2, :]

            def head_square(m, tile, need, count):
                act.wait_ge(need, count)
                nc.scalar.activation(res[:, 13:14, :], tile, ACT.Square).then_inc(hsq, 1)

            def head_root(m):
                act.wait_ge(htot, m + 1)
                if not isinstance(m, int) or m > 0:
                    act.wait_ge(roped, m)
                nc.scalar.activation(res[:, 14, :], ps[:, 7, :], ACT.Ln, scale=1.0 / HD,
                                     bias=eps[:]).then_inc(hlog, 1)
                act.wait_ge(hlog, m + 1)
                nc.scalar.activation(res[:, 14, :], res[:, 14, :], ACT.Exp, scale=-0.5).then_inc(hroot, 1)

            def op_split(out, in_, scale=1.0):
                copy(out[:, 0, :], in_, scale).then_inc(op_hi, 1)

            SA, SB = float(HD) ** -0.5, float(QK_B) ** -0.5

            def exps(n):
                for q in range(4):
                    act.wait_ge(max_done, n * 4 + q + 1)
                    if q == 0 and not (isinstance(n, int) and n == 0):
                        act.wait_ge(p_turned, n * 4)
                    nc.scalar.activation(res[:, PROB + q, :], ps[:, 4 + q, :], ACT.Exp, bias=negmax[:, q:q + 1],
                                         accum_out=psumrow[:, q:q + 1]).then_inc(exp_done, 1)

            def pt_split(n, kt, pt):
                act.wait_ge(p_turned, n * 4 + kt + 1)
                if kt == 3:
                    act.wait_ge(pv_done, n * 4 + 1)
                elif kt == 0 and not (isinstance(n, int) and n == 0):
                    act.wait_ge(pv_done, n * 4)
                copy(pt[kt % 3][:, 0, :], ps[:, PT_BANK[kt], :]).then_inc(pt_hi, 1)

            def o_split(n, out):
                act.wait_ge(pv_done, n * 4 + 4)
                copy(out, ps[:, 6:7, :]).then_inc(o_hi, 1)

            def ln_exp_table():
                nc.scalar.preload_act_table_set("natural_log_exp_and_others")

            act.dma_start(gn[:], gains).then_inc(gains_in, 16)
            ln_exp_table()
            def x_square(k):
                square(k, res[:, k, :], sq_a, u_hi, k + 1)

            for j in range(4):
                whi(j, j)
                if j == 0:
                    act.wait_ge(gains_in, 16)
                    act.wait_ge(x_first, 16)
                else:
                    act.wait_ge(x_in[j], 16)
                for k in range(4 * j, 4 * j + 4):
                    if k == 2:
                        act.wait_ge(x_in[0], 16)
                    copy(u_tile(k)[:, 0, :], res[:, k, :], gn[:, G_MIX + k:G_MIX + k + 1]).then_inc(u_hi, 1)
                if j:
                    x_square(2 * j - 2)
                    x_square(2 * j - 1)
            whi(4, 0)
            for k in range(6, 10):
                x_square(k)
            whi(5, 1)
            for k in range(10, 16):
                x_square(k)
            act.wait_ge(set_done, 1)
            whi(6, 2)
            whi(7, 3)
            root(0, 7, 0, D)
            whi(8, 0)
            whi(9, 1)
            for g in (2, 3):
                for j in range(4):
                    whi(4 * g + 2 + j, (2 + j) % 4)
            head_square(0, res[:, 8:9, :], emptied, 3)
            for m in range(3):
                b = 16 + 4 * m
                whi(b + 2, 2)
                head_root(m)
                whi(b + 3, 3)
                whi(b + 4, 0)
                act.wait_ge(roped, m + 1)
                op_split([K_A[0], K_A[1], Q_A][m], res[:, 15, :], SA if m == 2 else 1.0)
                if m < 2:
                    head_square(m + 1, res[:, [9, 0][m]:[10, 1][m], :], hnorm, m + 1)
                whi(b + 5, 1)
                if m < 2:
                    act.wait_ge(v_turned, m + 1)
                    op_split(V_A[m], ps[:, 4 + m, :])

            def gate_sigmoid(h, branch):
                t = tmp[:, 2 * branch:2 * branch + 2, :]
                act.wait_ge(emptied, h * 2 + G_GATE + branch + 1)
                nc.scalar.activation(t, t, ACT.Sigmoid).then_inc(gate_sig, 1)
                act.wait_ge(gate_sig, h * 2 + branch + 1)
                act.dma_start(gates[branch].rearrange("k p s -> p k s")[:, bass.ds(h * 2, 2), :],
                              t).then_inc(gate_out[branch], 16)

            def gqa_head(h, kv, more):
                b = h * 8 + N_GATE
                ln_exp_table()
                exps(h)
                if more:
                    head_square(h + 3, res[:, bass.ds(h + 1, 1), :], hnorm, h + 3)
                whi(b + 2, 2)
                whi(b + 3, 3)
                if more:
                    head_root(h + 3)
                whi(b + 4, 0)
                whi(b + 5, 1)
                pt_split(h, 0, PT_A)
                pt_split(h, 1, PT_A)
                if more:
                    act.wait_ge(roped, h + 4)
                    op_split(Q_A, res[:, 15, :], SA)
                gate_sigmoid(h, 0)
                whi(b + 6, 2)
                pt_split(h, 2, PT_A)
                pt_split(h, 3, PT_A)
                whi(b + 7, 3)
                o_split(h, r3[:, bass.ds(h, 1), 0, :])
                whi(b + 8, 0)
                whi(b + 9, 1)
                gate_sigmoid(h, 1)

            gqa_head(0, 0, True)
            with act.Fori(1, GROUP) as h:
                gqa_head(h, 0, True)
            with act.Fori(GROUP, HEADS - 1) as h:
                gqa_head(h, 1, True)
            gqa_head(HEADS - 1, 1, False)

            ln_exp_table()
            act.wait_ge(gate_out[1], 16 * HEADS)
            for g in range(4):
                for j in range(4):
                    whi(N_LAT + 4 * g + 2 + j, (2 + j) % 4)
                    if (g, j) == (3, 0):
                        root(1, 6, 1, LORA)
                for t in range(2):
                    k = 2 * g + t
                    act.wait_ge(emptied, G_LAT + g + 1)
                    copy(r2[:, k, 0, :], tmp[:, t, :], gn[:, G_QA + k:G_QA + k + 1]).then_inc(u_hi, 1)
                    square(16 + k, tmp[:, t, :], sq_a, emptied, G_LAT + g + 1)
            act.wait_ge(roped, 11)
            copy(KR_B[0:ROPE_B, 0, :], res[0:ROPE_B, 6, :]).then_inc(op_hi, 1)

            def mla_q_split(h):
                act.wait_ge(emptied, h * 2 + G_B + 1)
                act.wait_ge(scores, h * 4 + 4 * HEADS)
                op_split(Q_B, res[:, 0, :], SB)

            def mla_k_split(h):
                act.wait_ge(emptied, h * 2 + G_B + 2)
                op_split(K_B, res[:, 2, :])

            def mla_pe_split(h):
                act.wait_ge(roped, h + 12)
                copy(PE_B[0:ROPE_B, 0, :], res[0:ROPE_B, 6, :], SB).then_inc(op_hi, 1)

            def mla_v_split(h):
                act.wait_ge(v_turned, h + 3)
                act.wait_ge(pv_done, h * 4 + 4 * HEADS)
                op_split(V_B, ps[:, 0, :])

            whi(N_B + 2, 2)
            mla_q_split(0)
            root(2, 7, 2, LORA)
            mla_k_split(0)
            mla_pe_split(0)
            mla_v_split(0)
            whi(N_B + 3, 3)

            def mla_head(h, j0):
                n = h + HEADS
                b = h * 2 + N_B + 4
                exps(n)
                whi(b, j0)
                mla_q_split(h + 1)
                pt_split(n, 0, PT_B)
                pt_split(n, 1, PT_B)
                mla_k_split(h + 1)
                pt_split(n, 2, PT_B)
                pt_split(n, 3, PT_B)
                o_split(n, r0[:, bass.ds(h, 1), 0, :])
                mla_pe_split(h + 1)
                mla_v_split(h + 1)
                whi(b + 1, j0 + 1)

            with act.Fori(0, HEADS // 2 - 1) as i:
                mla_head(i * 2, 0)
                mla_head(i * 2 + 1, 2)
            mla_head(HEADS - 2, 0)

            def merge_a(pair):
                whi(pair * 4 + N_MERGE + 2, 2)
                whi(pair * 4 + N_MERGE + 3, 3)

            def merge_b(pair, out):
                whi(pair * 4 + N_MERGE + 4, 0)
                whi(pair * 4 + N_MERGE + 5, 1)
                act.wait_ge(mrg_sum, pair + 1)
                copy(out, tmp[:, 0:2, :]).then_inc(mrg_hi, 1)

            exps(15)
            whi(N_MERGE + 2, 2)
            for kt in range(3):
                pt_split(15, kt, PT_B)
            whi(N_MERGE + 3, 3)
            pt_split(15, 3, PT_B)
            o_split(15, r0[:, 7:8, 0, :])
            with act.Fori(0, 2) as i:
                for s in range(2):
                    merge_b(i * 2 + s, r1[:, bass.ds(i * 4 + 2 * s, 2), 0, :])
                    merge_a(i * 2 + s + 1)
            for pair in range(4, 8):
                merge_b(pair, r2[:, 2 * pair - 8:2 * pair - 6, 0, :])
                if pair < 7:
                    merge_a(pair + 1)

            ln_exp_table()
            for g in range(8):
                for j in range(4):
                    whi(N_WO + 4 * g + 2 + j, (2 + j) % 4)
                for t in range(2):
                    k = 2 * g + t
                    act.wait_ge(emptied, G_WO + g + 1)
                    copy(n_tile(k)[:, 0, :], res[:, k, :], gn[:, G_FFN + k:G_FFN + k + 1]).then_inc(u_hi, 1)
                    square(24 + k, res[:, k, :], sq_b, emptied, G_WO + g + 1)

            def ff_gate(g):
                act.wait_ge(emptied, g + 1)
                nc.scalar.activation(tmp[:, 0:2, :], tmp[:, 0:2, :], ACT.Silu).then_inc(ff_act, 1)

            def ff_hidden(e, half, down_before):
                act.wait_ge(ff_mul, e + 1)
                act.wait_ge(piece_used, down_before)
                copy(r1[:, 2 * half:2 * half + 2, 0, :], tmp[:, 2:4, :]).then_inc(ff_hi, 1)

            def four(n):
                for j in range(4):
                    whi(n + 2 + j, (2 + j) % 4)

            four(N_FF)
            root(3, 3, 0, D)
            nc.scalar.preload_act_table(ACT.Silu)
            ff_gate(G_FF)
            act.wait_ge(p_in, 16)
            for k in range(2):
                copy(P_T[k][:, 0, :], tab[:, 2 + k, :]).then_inc(u_hi, 1)

            def chunk(c, last):
                b, g = c * 24 + N_FF_LOOP, c * 12 + G_FF
                four(b)
                whi(b + 6, 2)
                ff_hidden(c * 2, 0, b)
                for j in range(3):
                    whi(b + 7 + j, (3 + j) % 4)
                ff_gate(g + 2)
                four(b + 8)
                if not last:
                    whi(b + 14, 2)
                    ff_hidden(c * 2 + 1, 1, b)
                    for j in range(3):
                        whi(b + 15 + j, (3 + j) % 4)
                    ff_gate(g + 4)
                    for d in range(8):
                        whi(b + 18 + d, (2 + d) % 4)
                else:
                    for i in range(4):
                        whi(b + 14 + i, (2 + i) % 4)
                        if i == 0:
                            ff_hidden(c * 2 + 1, 1, b)
                        if i:
                            three_squares(i - 1)

            def three_squares(slot):
                for i in range(3 * slot, min(3 * slot + 3, 32)):
                    k, g = i % 16, (G_E if i < 16 else G_D) + i % 16 // 2
                    square(40 + i, emb[:, k, :] if i < 16 else res[:, k, :], sq_b, emptied, g + 1)

            with act.Fori(0, CHUNKS - 1) as c:
                chunk(c, False)
            chunk(CHUNKS - 1, True)
            ln_exp_table()
            for d in range(8):
                whi(N_D + d + 2, (2 + d) % 4)
                three_squares(3 + d)
                for t in range(2):
                    k = 2 * d + t
                    act.wait_ge(emptied, G_D + d + 1)
                    copy(n_tile(k)[:, 0, :], res[:, k, :], gn[:, G_PLEN + k:G_PLEN + k + 1]).then_inc(u_hi, 1)
            def after_gate(g):
                for k in (2 * g, 2 * g + 1):
                    square(72 + k, res[:, k, :], sq_b, pg_res, g + 1)
                for k in (2 * g, 2 * g + 1):
                    copy(emb[:, k, :], res[:, k, :], gn[:, G_FIN + k:G_FIN + k + 1]).then_inc(gained, 1)

            for g in range(8):
                b = N_PLE + 4 * g
                if g != 1:
                    whi(b + 2, 2)
                whi(b + 3, 3)
                if g:
                    after_gate(g - 1)
                if g < 7:
                    whi(b + 4, 0)
                    whi(b + 5, 1)
                if g == 0:
                    root(4, 3, 2, D)
                    root(5, 2, 1, D)
                    whi(b + 6, 2)
                if g < 7:
                    act.wait_ge(emptied, G_PLE + g + 1)
                    nc.scalar.activation(tmp[:, 0:2, :], tmp[:, 0:2, :], ACT.Sigmoid).then_inc(pg_sig, 1)
            for t in range(2):
                act.wait_ge(tail_emptied, t + 1)
                nc.scalar.activation(tmp[:, t, :], tmp[:, t, :], ACT.Sigmoid).then_inc(pg_sig, 1)
                square(86 + t, res[:, 14 + t, :], sq_b, tail_res, t + 1)
            ln_exp_table()
            root(6, TAIL_BANK, 0, D)
            for k in (14, 15):
                copy(emb[:, k, :], res[:, k, :], gn[:, G_FIN + k:G_FIN + k + 1]).then_inc(gained, 1)

        @block.vector
        def _(dve):
            tt = nc.vector.tensor_tensor
            sq_b = tab[:, 0:2, :]
            stt = nc.vector.scalar_tensor_tensor

            def wlo(n, j):
                dve.wait_ge(w_hi_done, n + 1)
                tt(w_lo[:, j % HL], raw[:, j], w_hi[:, j % HL], ALU.subtract).then_inc(w_lo_done, 1)

            def four(n):
                for j in range(4):
                    wlo(n + 2 + j, (2 + j) % 4)

            def both(r):
                return rstd[:, r:r + 1, :].broadcast_to([P, 2, SEQ])

            def empty(out, bank, r, n):
                dve.wait_ge(piece_used, n + 1)
                tt(out, ps[:, bank:bank + 2, :], both(r), ALU.mult).then_inc(emptied, 1)

            def refined(r, w, total_of, width, log, root, turn, count, done):
                base = turn * (4 if done is count else 3)
                dve.wait_ge(log, turn + 1)
                nc.vector.tensor_scalar(w, total_of, 1.0 / width, EPS, ALU.mult, ALU.add).then_inc(count, 1)
                dve.wait_ge(root, turn + 1)
                dve.wait_ge(count, base + 1)
                tt(w, w, r, ALU.mult).then_inc(count, 1)
                dve.wait_ge(count, base + 2)
                stt(w, w, -0.5, r, ALU.mult, ALU.mult).then_inc(count, 1)
                dve.wait_ge(count, base + 3)
                stt(r, w, 1.5, r, ALU.add, ALU.mult).then_inc(done, 1)

            def recip(turn, norm, bank, r, width):
                refined(rstd[:, r, :], sums(norm), ps[:, bank, :], width, log_done, root_done, turn, refine,
                        rstd_done)
                dve.wait_ge(rstd_done, turn + 1)

            def gain_lo(out, in_, gain, n):
                dve.wait_ge(u_hi, n + 1)
                stt(out[:, 1, :], in_, gn[:, gain:gain + 1], out[:, 0, :], ALU.mult, ALU.subtract).then_inc(u_lo, 1)

            def head_norm(m, tile, gain):
                refined(res[:, 14, :], res[:, 13, :], ps[:, 7, :], HD, hlog, hroot, m, hrefine, hrefine)
                dve.wait_ge(hrefine, m * 4 + 4)
                stt(tile, tile, gn[:, gain:gain + 1], res[:, 14:15, :], ALU.mult, ALU.mult).then_inc(hnorm, 1)

            def rotate(m, tile, cs, tc, ts_, rows, before, bank=7):
                if not isinstance(before, int) or before:
                    dve.wait_ge(op_hi, before)
                    dve.wait_ge(op_lo, before)
                tt(tc, tile, tab[0:rows, cs:cs + 1, :], ALU.mult).then_inc(by_cos, 1)
                dve.wait_ge(swapped, m + 1)
                tt(ts_, ps[0:rows, bank:bank + 1, :], tab[0:rows, cs + 1:cs + 2, :], ALU.mult).then_inc(by_sin, 1)
                dve.wait_ge(by_cos, m + 1)
                dve.wait_ge(by_sin, m + 1)
                tt(tc, tc, ts_, ALU.add).then_inc(roped, 1)

            def op_split(idx, out, in_, scale=None):
                dve.wait_ge(op_hi, idx + 1)
                if scale is None:
                    tt(out[:, 1, :], in_, out[:, 0, :], ALU.subtract).then_inc(op_lo, 1)
                else:
                    stt(out[:, 1, :], in_, scale, out[:, 0, :], ALU.mult, ALU.subtract).then_inc(op_lo, 1)

            SA, SB = float(HD) ** -0.5, float(QK_B) ** -0.5

            def softmax(n):
                for q in range(4):
                    dve.wait_ge(scores, n * 4 + q + 1)
                    nc.vector.tensor_reduce(negmax[:, q:q + 1], ps[:, 4 + q, :], AX_X, ALU.max,
                                            negate=True).then_inc(max_done, 1)
                for q in range(4):
                    dve.wait_ge(exp_done, n * 4 + q + 1)
                    nc.vector.reciprocal(rrow[:, q:q + 1], psumrow[:, q:q + 1]).then_inc(rsum_done, 1)
                    dve.wait_ge(rsum_done, n * 4 + q + 1)
                    nc.vector.tensor_scalar(res[:, PROB + q, :], res[:, PROB + q, :], rrow[:, q:q + 1], None,
                                            ALU.mult).then_inc(p_done, 1)

            def pt_split(n, kt, pt):
                dve.wait_ge(pt_hi, n * 4 + kt + 1)
                tt(pt[kt % 3][:, 1, :], ps[:, PT_BANK[kt], :], pt[kt % 3][:, 0, :], ALU.subtract).then_inc(pt_lo, 1)

            def o_split(n, out):
                dve.wait_ge(o_hi, n + 1)
                tt(out[:, :, 1, :], ps[:, 6:7, :], out[:, :, 0, :], ALU.subtract).then_inc(o_lo, 1)

            nc.vector.memset(eps[:], EPS).then_inc(set_done, 1)
            dve.wait_ge(gains_in, 16)
            for k in range(KD):
                if k % 4 == 0:
                    wlo(k // 4, k // 4)
                gain_lo(u_tile(k), res[:, k, :], G_MIX + k, k)
            for n in range(4, 8):
                wlo(n, n % 4)
            recip(0, 0, 7, 0, D)
            dve.wait_ge(sq_done, 16)
            dve.wait_ge(u_lo, 16)
            empty(res[:, 8:10, :], 0, 0, 3)
            wlo(8, 0)
            wlo(9, 1)
            empty(res[:, 10:12, :], 2, 0, 7)
            four(8)
            dve.wait_ge(piece_used, 12)
            tt(res[:, 12, :], ps[:, 0, :], rstd[:, 0, :], ALU.mult).then_inc(emptied, 1)
            four(12)
            empty(res[:, 0:2, :], 2, 0, 15)
            dve.wait_ge(tables_in, 16)
            dve.wait_ge(emptied, 4)
            for m, (t, gain) in enumerate(((8, G_KN), (9, G_KN), (0, G_QN))):
                b = 16 + 4 * m
                wlo(b + 2, 2)
                head_norm(m, res[:, t:t + 1, :], gain)
                wlo(b + 3, 3)
                wlo(b + 4, 0)
                dve.wait_ge(hnorm, m + 1)
                rotate(m, res[:, t:t + 1, :], 0, res[:, 15:16, :], res[:, 14:15, :], P, 2 * m)
                dve.wait_ge(roped, m + 1)
                op_split(2 * m, [K_A[0], K_A[1], Q_A][m], res[:, 15, :], SA if m == 2 else None)
                wlo(b + 5, 1)
                if m < 2:
                    op_split(2 * m + 1, V_A[m], ps[:, 4 + m, :])
                empty(res[:, 2 + 2 * m:4 + 2 * m, :], 2 * (m % 2), 0, b + 3)

            def gate_group(h, branch, n):
                if not isinstance(h, int) or h > 0:
                    dve.wait_ge(gate_out[branch], h * 16)
                empty(tmp[:, 2 * branch:2 * branch + 2, :], 2 - 2 * branch, 0, n)

            def gqa_head(h, kv, more):
                b = h * 8 + N_GATE
                tile = res[:, bass.ds(h + 1, 1), :] if more else None
                softmax(h)
                wlo(b + 2, 2)
                wlo(b + 3, 3)
                if more:
                    head_norm(h + 3, tile, G_QN)
                wlo(b + 4, 0)
                wlo(b + 5, 1)
                if more:
                    dve.wait_ge(hnorm, h + 4)
                    rotate(h + 3, tile, 0, res[:, 15:16, :], res[:, 14:15, :], P, h + 5)
                pt_split(h, 0, PT_A)
                pt_split(h, 1, PT_A)
                gate_group(h, 0, b + 3)
                if more:
                    dve.wait_ge(roped, h + 4)
                    op_split(h + 5, Q_A, res[:, 15, :], SA)
                wlo(b + 6, 2)
                pt_split(h, 2, PT_A)
                pt_split(h, 3, PT_A)
                wlo(b + 7, 3)
                o_split(h, r3[:, bass.ds(h, 1)])
                wlo(b + 8, 0)
                wlo(b + 9, 1)
                gate_group(h, 1, b + 7)

            gqa_head(0, 0, True)
            with dve.Fori(1, GROUP) as h:
                gqa_head(h, 0, True)
            with dve.Fori(GROUP, HEADS - 1) as h:
                gqa_head(h, 1, True)
            gqa_head(HEADS - 1, 1, False)

            kr = slice(0, ROPE_B)
            dve.wait_ge(gate_out[0], 16 * HEADS)
            for g in range(4):
                for j in range(4):
                    wlo(N_LAT + 4 * g + 2 + j, (2 + j) % 4)
                    if (g, j) == (3, 1):
                        recip(1, 1, 6, 1, LORA)
                if g:
                    dve.wait_ge(u_hi, 16 + 2 * g)
                    dve.wait_ge(u_lo, 16 + 2 * g)
                    dve.wait_ge(sq_done, 16 + 2 * g)
                empty(tmp[:, 0:2, :], 2 * ((G_LAT + g) % 2), 0, N_LAT + 4 * g + 3)
                for t in range(2):
                    k = 2 * g + t
                    gain_lo(r2[:, k], tmp[:, t, :], G_QA + k, 16 + k)
                if g == 0:
                    rotate(10, res[kr, 12:13, :], 2, res[kr, 6:7, :], res[kr, 7:8, :], ROPE_B, OP_KR)
            dve.wait_ge(roped, 11)
            op_split(OP_KR, KR_B[kr], res[kr, 6, :])

            def mla_q(h):
                dve.wait_ge(op_hi, h * 4 + OP_B)
                dve.wait_ge(op_lo, h * 4 + OP_B)
                empty(res[:, 0:2, :], 2, 1, h * 2 + N_B)

            def mla_kv(h):
                empty(res[:, 2:4, :], 0, 2, h * 2 + N_B + 1)

            def mla_rotate(h):
                dve.wait_ge(emptied, h * 2 + G_B + 1)
                rotate(h + 11, res[kr, 1:2, :], 2, res[kr, 6:7, :], res[kr, 7:8, :], ROPE_B, h * 4 + OP_B, 2)

            def mla_q_lo(h):
                dve.wait_ge(emptied, h * 2 + G_B + 1)
                op_split(h * 4 + OP_B, Q_B, res[:, 0, :], SB)

            def mla_k_lo(h):
                dve.wait_ge(emptied, h * 2 + G_B + 2)
                op_split(h * 4 + OP_B + 1, K_B, res[:, 2, :])

            def mla_pe_lo(h):
                dve.wait_ge(roped, h + 12)
                op_split(h * 4 + OP_B + 2, PE_B[kr], res[kr, 6, :], SB)

            def mla_v_lo(h):
                op_split(h * 4 + OP_B + 3, V_B, ps[:, 0, :])

            mla_q(0)
            wlo(N_B + 2, 2)
            mla_q_lo(0)
            recip(2, 2, 7, 2, LORA)
            mla_kv(0)
            mla_k_lo(0)
            mla_rotate(0)
            mla_pe_lo(0)
            mla_v_lo(0)
            wlo(N_B + 3, 3)

            def mla_head(h, j0):
                n = h + HEADS
                b = h * 2 + N_B + 4
                softmax(n)
                mla_q(h + 1)
                wlo(b, j0)
                mla_q_lo(h + 1)
                mla_kv(h + 1)
                pt_split(n, 0, PT_B)
                pt_split(n, 1, PT_B)
                mla_k_lo(h + 1)
                pt_split(n, 2, PT_B)
                pt_split(n, 3, PT_B)
                mla_rotate(h + 1)
                o_split(n, r0[:, bass.ds(h, 1)])
                mla_pe_lo(h + 1)
                mla_v_lo(h + 1)
                wlo(b + 1, j0 + 1)

            with dve.Fori(0, HEADS // 2 - 1) as i:
                mla_head(i * 2, 0)
                mla_head(i * 2 + 1, 2)
            mla_head(HEADS - 2, 0)

            def gated(out, bank, gate, n):
                dve.wait_ge(piece_used, n + 1)
                tt(out, ps[:, bank:bank + 2, :], gate, ALU.mult).then_inc(emptied, 1)

            def merge_a(pair, s):
                n = pair * 4 + N_MERGE
                if isinstance(pair, int) and pair == 0:
                    wlo(n + 2, 2)
                    for kt in range(3):
                        pt_split(15, kt, PT_B)
                    wlo(n + 3, 3)
                    pt_split(15, 3, PT_B)
                else:
                    wlo(n + 2, 2)
                    wlo(n + 3, 3)
                dve.wait_ge(gate_in[s], pair * 16 + 32 - 16 * s)
                dve.wait_ge(w_lo_done, n + 4)
                gated(tmp[:, 0:2, :], 2, res[:, GATE_IN[s]:GATE_IN[s] + 2, :], n + 1)

            def merge_b(pair, s, out):
                n = pair * 4 + N_MERGE
                wlo(n + 4, 0)
                wlo(n + 5, 1)
                gated(tmp[:, 2:4, :], 0, res[:, GATE_IN[s] + 2:GATE_IN[s] + 4, :], n + 3)
                dve.wait_ge(mrg_hi, pair + 1)
                tt(out[:, :, 1, :], tmp[:, 0:2, :], out[:, :, 0, :], ALU.subtract).then_inc(mrg_lo, 1)

            softmax(15)
            merge_a(0, 0)
            o_split(15, r0[:, 7:8])
            with dve.Fori(0, 2) as i:
                for s in range(2):
                    merge_b(i * 2 + s, s, r1[:, bass.ds(i * 4 + 2 * s, 2)])
                    merge_a(i * 2 + s + 1, 1 - s)
            for pair in range(4, 8):
                merge_b(pair, pair % 2, r2[:, 2 * pair - 8:2 * pair - 6])
                if pair < 7:
                    merge_a(pair + 1, (pair + 1) % 2)

            def add_residual(d, pair, n):
                dve.wait_ge(piece_used, n + 1)
                r = res[:, 2 * d:2 * d + 2, :]
                tt(r, ps[:, 2 * pair:2 * pair + 2, :], r, ALU.add).then_inc(emptied, 1)

            for g in range(8):
                four(N_WO + 4 * g)
                dve.wait_ge(x_again[g // 4], 16)
                add_residual(g, (G_WO + g) % 2, N_WO + 4 * g + 3)
                dve.wait_ge(emptied, G_WO + g + 1)
                for k in (2 * g, 2 * g + 1):
                    gain_lo(n_tile(k), res[:, k, :], G_FFN + k, 24 + k)

            def ff_lo_part(e, half):
                dve.wait_ge(ff_hi, e + 1)
                tt(r1[:, 2 * half:2 * half + 2, 1, :], tmp[:, 2:4, :], r1[:, 2 * half:2 * half + 2, 0, :],
                   ALU.subtract).then_inc(ff_lo, 1)

            four(N_FF)
            recip(3, 3, 3, 0, D)
            empty(tmp[:, 0:2, :], 4, 0, N_FF + 3)

            def chunk(c, last):
                b, g = c * 24 + N_FF_LOOP, c * 12 + G_FF
                four(b)
                if isinstance(c, int) and c == 0:
                    dve.wait_ge(p_in, 16)
                    for k in range(2):
                        dve.wait_ge(u_hi, 41 + k)
                        tt(P_T[k][:, 1, :], tab[:, 2 + k, :], P_T[k][:, 0, :], ALU.subtract).then_inc(u_lo, 1)
                else:
                    dve.wait_ge(ff_lo, c * 2)
                empty(tmp[:, 2:4, :], 6, 0, b + 3)
                wlo(b + 6, 2)
                ff_lo_part(c * 2, 0)
                for j in range(3):
                    wlo(b + 7 + j, (3 + j) % 4)
                dve.wait_ge(ff_mul, c * 2 + 1)
                empty(tmp[:, 0:2, :], 0, 0, b + 7)
                four(b + 8)
                dve.wait_ge(ff_lo, c * 2 + 1)
                empty(tmp[:, 2:4, :], 2, 0, b + 11)
                if not last:
                    wlo(b + 14, 2)
                    ff_lo_part(c * 2 + 1, 1)
                    for j in range(3):
                        wlo(b + 15 + j, (3 + j) % 4)
                    dve.wait_ge(ff_mul, c * 2 + 2)
                    empty(tmp[:, 0:2, :], 4, 0, b + 15)
                    dve.wait_ge(emptied, g + 1)
                    for d in range(8):
                        wlo(b + 18 + d, (2 + d) % 4)
                        add_residual(d, (3 + d) % 4, b + 16 + d)
                else:
                    for i in range(4):
                        wlo(b + 14 + i, (2 + i) % 4)
                        if i == 0:
                            ff_lo_part(c * 2 + 1, 1)
                        for e in (2 * i, 2 * i + 1):
                            if e % 2:
                                dve.wait_ge(piece_used, N_E + i + 1)
                            else:
                                dve.wait_ge(emb_group, i + 1)
                            bank = 2 * ff_pair(G_E + e)
                            nc.vector.tensor_copy(emb[:, 2 * e:2 * e + 2, :],
                                                  ps[:, bank:bank + 2, :]).then_inc(emptied, 1)

            chunk(0, False)
            with dve.Fori(1, CHUNKS - 1) as c:
                chunk(c, False)
            chunk(CHUNKS - 1, True)
            for d in range(8):
                wlo(N_D + 2 + d, (2 + d) % 4)
                add_residual(d, ff_pair(G_D + d), N_D + d)
                dve.wait_ge(emptied, G_D + d + 1)
                for k in (2 * d, 2 * d + 1):
                    gain_lo(n_tile(k), res[:, k, :], G_PLEN + k, 42 + k)
            for g in range(8):
                for j in range(1 if g == 1 else 0, 4 if g < 7 else 2):
                    wlo(N_PLE + 4 * g + 2 + j, (2 + j) % 4)
                if g == 0:
                    recip(4, 5, 3, 2, D)
                if g:
                    dve.wait_ge(pg_res, g)
                if g < 7:
                    empty(tmp[:, 0:2, :], 2 * ff_pair(G_PLE + g), 2, N_PLE + 4 * g + 3)
                if g == 0:
                    wlo(N_PLE + 6, 2)
                    recip(5, 4, 2, 1, D)
                for k in (2 * g, 2 * g + 1):
                    stt(emb[:, k, :], emb[:, k, :], gn[:, G_POST + k:G_POST + k + 1], rstd[:, 1, :],
                        ALU.mult, ALU.mult).then_inc(emb_normed, 1)
            def tail_empty(t):
                dve.wait_ge(tail_tile, t + 1)
                tt(tmp[:, t, :], ps[:, 2 * ff_pair(G_PLE + 7) + t, :], rstd[:, 2, :], ALU.mult).then_inc(tail_emptied, 1)

            def tail_add(t):
                dve.wait_ge(pg_sig, 8 + t)
                dve.wait_ge(emb_normed, 16)
                tt(tmp[:, t, :], tmp[:, t, :], emb[:, 14 + t, :], ALU.mult).then_inc(tail_mul, 1)
                dve.wait_ge(tail_mul, t + 1)
                tt(res[:, 14 + t, :], res[:, 14 + t, :], tmp[:, t, :], ALU.add).then_inc(tail_res, 1)

            tail_empty(0)
            tail_add(0)
            tail_empty(1)
            dve.wait_ge(sq_done, 87)
            dve.wait_ge(acc_done, 86)
            tt(acc[:], acc[:], sq_b[:, 0, :], ALU.add).then_inc(acc_done, 1)
            tail_add(1)
            recip(6, 6, TAIL_BANK, 0, D)
            for k in range(FIN_POOL, KD, 2):
                dve.wait_ge(gained, k + 2)
                tt(emb[:, k:k + 2, :], emb[:, k:k + 2, :], both(0), ALU.mult).then_inc(fin_dve, 1)

        @block.gpsimd
        def _(pool):
            def add_square(s, first, norm, sq):
                out = sums(norm)
                pool.wait_ge(sq_done, s + 1)
                if s == first:
                    if norm == 4:
                        pool.wait_ge(u_lo, 42)
                    elif norm:
                        pool.wait_ge(rstd_done, 4 if norm == 5 else norm)
                    nc.gpsimd.tensor_copy(out, sq[:, s % 2, :]).then_inc(acc_done, 1)
                else:
                    pool.wait_ge(acc_done, s)
                    nc.gpsimd.tensor_tensor(out, out, sq[:, s % 2, :], ALU.add).then_inc(acc_done, 1)

            sq_a, sq_b = tmp[:, 2:4, :], tab[:, 0:2, :]
            for norm, first, end in ((0, 0, 16), (1, 16, 20), (2, 20, 24)):
                for s in range(first, end):
                    add_square(s, first, norm, sq_a)

            with pool.Fori(0, 8) as i:
                pool.wait_ge(emptied, i * 2 + G_MERGE + 2)
                nc.gpsimd.tensor_tensor(tmp[:, 0:2, :], tmp[:, 0:2, :], tmp[:, 2:4, :], ALU.add).then_inc(mrg_sum, 1)
            for s in range(24, 40):
                add_square(s, 24, 3, sq_b)
            with pool.Fori(0, CHUNKS) as c:
                for half in range(2):
                    pool.wait_ge(emptied, c * 12 + G_FF + 2 + 2 * half)
                    pool.wait_ge(ff_act, c * 2 + half + 1)
                    nc.gpsimd.tensor_tensor(tmp[:, 2:4, :], tmp[:, 2:4, :], tmp[:, 0:2, :],
                                            ALU.mult).then_inc(ff_mul, 1)
            for norm, first in ((4, 40), (5, 56)):
                for s in range(first, first + 16):
                    add_square(s, first, norm, sq_b)
            for g in range(7):
                pool.wait_ge(pg_sig, g + 1)
                pool.wait_ge(emb_normed, 2 * g + 2)
                nc.gpsimd.tensor_tensor(tmp[:, 0:2, :], tmp[:, 0:2, :], emb[:, 2 * g:2 * g + 2, :],
                                        ALU.mult).then_inc(pg_mul, 1)
                pool.wait_ge(pg_mul, g + 1)
                if g == 0:
                    pool.wait_ge(u_hi, 58)
                    pool.wait_ge(u_lo, 58)
                    pool.wait_ge(sq_done, 72)
                r = res[:, 2 * g:2 * g + 2, :]
                nc.gpsimd.tensor_tensor(r, r, tmp[:, 0:2, :], ALU.add).then_inc(pg_res, 1)
                for s in (72 + 2 * g, 73 + 2 * g):
                    add_square(s, 72, 6, sq_b)
            pool.wait_ge(rstd_done, 7)
            pool.wait_ge(gained, FIN_POOL)
            for k in range(0, FIN_POOL, 2):
                nc.gpsimd.tensor_tensor(emb[:, k:k + 2, :], emb[:, k:k + 2, :],
                                        rstd[:, 0:1, :].broadcast_to([P, 2, SEQ]), ALU.mult).then_inc(fin_pool, 1)


INPUTS = ["xT", "pT", "gains", "tables", "mats", "w_in", "w_qb", "w_kvb", "w_a", "w_b", "w_o", "w_gu", "w_dn",
          "w_pg", "w_pp"]


def rotary_tables():
    s = np.arange(SEQ)
    out = np.zeros((P, 4, SEQ), np.float32)
    for i, d in enumerate((HD, ROPE_B)):
        half, n2 = d // 2, d // 4
        inv = (1.0 / (np.float32(THETA) ** (np.arange(0, half, 2, dtype=np.float32) / np.float32(half)))
               ).astype(np.float32)
        for f in range(d):
            pos = (s // GRID_W if f < half else s % GRID_W).astype(np.float32)
            ang = pos * inv[f % n2]
            out[f, 2 * i] = np.cos(ang)
            out[f, 2 * i + 1] = np.sin(ang) * np.float32(-1.0 if f % half < n2 else 1.0)
    return out


def matrices():
    out = np.zeros((P, 4, P), np.float32)
    i = np.arange(P)
    out[i, 0, i] = 1.0
    out[:, 1, :] = 1.0
    out[i, 2, i ^ (HD // 4)] = 1.0
    out[i, 3, i ^ (ROPE_B // 4)] = 1.0
    return out


def kernel(**inputs):
    import concourse.bacc as _bacc
    from concourse.bass_utils import run_bass_kernel_spmd as _run

    a = {k: np.asarray(v) for k, v in inputs.items()}
    tiles = ("g_mix", "g_ffn", "g_ple", "g_ple_post", "g_final", "q_a_norm", "kv_a_norm", "q_norm_a", "k_norm_a")
    given = {
        "xT": a["x"][0].T, "pT": a["p"][0, 0].T,
        "gains": np.concatenate([a[k].reshape(-1, P).T for k in tiles], axis=1),
        "tables": rotary_tables(), "mats": matrices(),
        "w_in": a["w_in"][0], "w_qb": a["w_q_b"][0], "w_kvb": a["w_kv_b"][0], "w_a": a["w_a_out"][0],
        "w_b": a["w_b_out"][0], "w_o": a["w_o"][0], "w_gu": a["w_gate_up"][0], "w_dn": a["w_down"][0],
        "w_pg": a["w_ple_gate"][0], "w_pp": a["w_ple_proj"][0],
    }
    given = {k: np.ascontiguousarray(v) for k, v in given.items()}
    nc = _bacc.Bacc("TRN2", target_bir_lowering=False, num_devices=1, dynamic_dma_scratch_size=1024)
    args = [nc.dram_tensor(k, given[k].shape, F32, kind="ExternalInput").ap() for k in INPUTS]
    out = nc.dram_tensor("outT", (D, SEQ), F32, kind="ExternalOutput").ap()
    build(nc, *args, out)
    r = _run(nc, [{k: given[k] for k in INPUTS}], core_ids=[0])
    return np.ascontiguousarray(r.results[0]["outT"].T)[None]
```
